# Optimizing a Trainium2 kernel written in Bass

```python
import jax
import jax.numpy as jnp
from jax import lax
import numpy as np

D_MODEL = 1024
BATCH = 1
SEQ = 256
DEPTH = 2

N_HEADS = 16
HEAD_DIM = D_MODEL // N_HEADS
ROPE_DIM = HEAD_DIM // 4
ROPE_THETA = 500000.0
NSA_KV_HEADS = 4
NSA_GROUP = N_HEADS // NSA_KV_HEADS
CMP_BLOCK = 32
CMP_STRIDE = 16
CMP_HIDDEN = 256
SEL_BLOCK = 64
SEL_TOPK = 16
WINDOW = 512
NSA_Q_CHUNK = 128
NSA_Q_DIM = N_HEADS * HEAD_DIM
NSA_KV_DIM = NSA_KV_HEADS * HEAD_DIM
NSA_IN = NSA_Q_DIM + 6 * NSA_KV_DIM + 3 * N_HEADS
MOBA_BLOCK = 256
MOBA_TOPK = 3
MOBA_Q_CHUNK = 64
D_FF = -(-8 * D_MODEL // (3 * 256)) * 256
ALPHA = (2 * DEPTH) ** 0.25
BETA = (8 * DEPTH) ** -0.25
N_NSA = (DEPTH + 1) // 2
N_MOBA = DEPTH // 2
LN_EPS = 1e-5
LARGE = 1e30

kernel_name = 'hybrid_nsa_moba_deepnorm'

def rope_partial(x, pos):
    inv = ROPE_THETA ** (-jnp.arange(0, ROPE_DIM, 2, dtype=jnp.float32) / ROPE_DIM)
    ang = pos.astype(jnp.float32)[..., None] * inv
    cos = jnp.cos(ang)[:, :, None, :]
    sin = jnp.sin(ang)[:, :, None, :]
    xr = x[..., :ROPE_DIM].astype(jnp.float32)
    x1, x2 = xr[..., :ROPE_DIM // 2], xr[..., ROPE_DIM // 2:]
    rot = jnp.concatenate([x1 * cos - x2 * sin, x2 * cos + x1 * sin], axis=-1).astype(x.dtype)
    return jnp.concatenate([rot, x[..., ROPE_DIM:]], axis=-1)

def masked_softmax(s, mask):
    return jax.nn.softmax(jnp.where(mask, s, -LARGE), axis=-1)

def layer_norm(x, g, b):
    xf = x.astype(jnp.float32)
    mu = jnp.mean(xf, axis=-1, keepdims=True)
    var = jnp.mean(jnp.square(xf - mu), axis=-1, keepdims=True)
    y = (xf - mu) * lax.rsqrt(var + LN_EPS)
    return (y * g + b).astype(x.dtype)

def compress(k, pos_emb, w1, w2):
    B, S, G, hd = k.shape
    n_cmp = (S - CMP_BLOCK) // CMP_STRIDE + 1
    idx = jnp.arange(n_cmp)[:, None] * CMP_STRIDE + jnp.arange(CMP_BLOCK)[None, :]
    blocks = k[:, idx] + pos_emb[None, None, :, None, :]
    blocks = blocks.transpose(0, 3, 1, 2, 4).reshape(B, G, n_cmp, CMP_BLOCK * hd)
    return jax.nn.gelu(blocks @ w1) @ w2

def nsa_mixer(h, pos, w_in, w_o, ck_pos, ck_w1, ck_w2, cv_pos, cv_w1, cv_w2):
    B, S, _ = h.shape
    G, R, hd, CH = NSA_KV_HEADS, NSA_GROUP, HEAD_DIM, NSA_Q_CHUNK
    proj = h @ w_in
    q = rope_partial(proj[..., :NSA_Q_DIM].reshape(B, S, N_HEADS, hd), pos).reshape(B, S, G, R, hd)
    kv = proj[..., NSA_Q_DIM:NSA_Q_DIM + 6 * NSA_KV_DIM].reshape(B, S, 6, G, hd)
    gates = jax.nn.sigmoid(proj[..., NSA_Q_DIM + 6 * NSA_KV_DIM:].astype(jnp.float32)).reshape(B, S, G, R, 3)
    k_cmp = rope_partial(kv[:, :, 0], pos)
    v_cmp = kv[:, :, 1]
    k_sel = rope_partial(kv[:, :, 2], pos)
    v_sel = kv[:, :, 3]
    k_win = rope_partial(kv[:, :, 4], pos)
    v_win = kv[:, :, 5]

    kc = compress(k_cmp, ck_pos, ck_w1, ck_w2)
    vc = compress(v_cmp, cv_pos, cv_w1, cv_w2)
    n_cmp = kc.shape[2]
    cmp_start = jnp.arange(n_cmp) * CMP_STRIDE
    cmp_end = cmp_start + CMP_BLOCK - 1
    n_sel = S // SEL_BLOCK
    n_top = min(SEL_TOPK, n_sel)
    sel_ids = jnp.arange(n_sel)
    sel_start = sel_ids * SEL_BLOCK
    lo = jnp.maximum(cmp_start[:, None], sel_start[None, :])
    hi = jnp.minimum(cmp_end[:, None], sel_start[None, :] + SEL_BLOCK - 1)
    overlap = jnp.clip(hi - lo + 1, 0, None).astype(jnp.float32) / CMP_STRIDE

    ks_blk = k_sel.reshape(B, n_sel, SEL_BLOCK, G, hd).transpose(0, 3, 1, 2, 4)
    vs_blk = v_sel.reshape(B, n_sel, SEL_BLOCK, G, hd).transpose(0, 3, 1, 2, 4)
    kw_pad = jnp.pad(k_win, ((0, 0), (WINDOW, 0), (0, 0), (0, 0)))
    vw_pad = jnp.pad(v_win, ((0, 0), (WINDOW, 0), (0, 0), (0, 0)))
    scale = HEAD_DIM ** -0.5
    b_ix = jnp.arange(B)[:, None, None, None]
    g_ix = jnp.arange(G)[None, :, None, None]

    def step(c):
        qs = c * CH
        tq = qs + jnp.arange(CH)
        qc = lax.dynamic_slice_in_dim(q, qs, CH, axis=1)
        gc = lax.dynamic_slice_in_dim(gates, qs, CH, axis=1)
        s = jnp.einsum('bqgrd,bgnd->bgrqn', qc, kc).astype(jnp.float32) * scale
        m = cmp_end[None, :] <= tq[:, None]
        p_cmp = masked_softmax(s, m) * jnp.any(m, axis=-1)[:, None]
        o_cmp = jnp.einsum('bgrqn,bgnd->bqgrd', p_cmp.astype(vc.dtype), vc)
        imp = jnp.einsum('bgrqn,nj->bgqj', p_cmp, overlap)
        blk = tq // SEL_BLOCK
        causal = sel_start[None, :] <= tq[:, None]
        forced = (sel_ids[None, :] == 0) | (sel_ids[None, :] == blk[:, None]) | (sel_ids[None, :] == blk[:, None] - 1)
        score = jnp.where(forced, LARGE, jnp.where(causal, imp, -LARGE))
        _, sel = lax.top_k(score, n_top)
        kg = ks_blk[b_ix, g_ix, sel].reshape(B, G, CH, n_top * SEL_BLOCK, hd)
        vg = vs_blk[b_ix, g_ix, sel].reshape(B, G, CH, n_top * SEL_BLOCK, hd)
        kpos = sel[..., None] * SEL_BLOCK + jnp.arange(SEL_BLOCK)
        msel = (kpos <= tq[:, None, None]).reshape(B, G, 1, CH, n_top * SEL_BLOCK)
        s = jnp.einsum('bqgrd,bgqkd->bgrqk', qc, kg).astype(jnp.float32) * scale
        p = masked_softmax(s, msel)
        o_sel = jnp.einsum('bgrqk,bgqkd->bqgrd', p.astype(vg.dtype), vg)
        kwc = lax.dynamic_slice_in_dim(kw_pad, qs, CH + WINDOW, axis=1)
        vwc = lax.dynamic_slice_in_dim(vw_pad, qs, CH + WINDOW, axis=1)
        kpos_w = qs - WINDOW + jnp.arange(CH + WINDOW)
        dist = tq[:, None] - kpos_w[None, :]
        mw = (kpos_w[None, :] >= 0) & (dist >= 0) & (dist < WINDOW)
        s = jnp.einsum('bqgrd,bkgd->bgrqk', qc, kwc).astype(jnp.float32) * scale
        p = masked_softmax(s, mw)
        o_win = jnp.einsum('bgrqk,bkgd->bqgrd', p.astype(vwc.dtype), vwc)
        o = gc[..., 0:1] * o_cmp + gc[..., 1:2] * o_sel + gc[..., 2:3] * o_win
        return o.reshape(B, CH, NSA_Q_DIM).astype(h.dtype)

    out = lax.map(step, jnp.arange(S // CH))
    out = out.transpose(1, 0, 2, 3).reshape(B, S, NSA_Q_DIM)
    return out @ w_o

def moba_mixer(h, pos, w_in, w_o):
    B, S, _ = h.shape
    H, hd, CH, BLK = N_HEADS, HEAD_DIM, MOBA_Q_CHUNK, MOBA_BLOCK
    proj = h @ w_in
    q = rope_partial(proj[..., :D_MODEL].reshape(B, S, H, hd), pos)
    k = rope_partial(proj[..., D_MODEL:2 * D_MODEL].reshape(B, S, H, hd), pos)
    v = proj[..., 2 * D_MODEL:].reshape(B, S, H, hd)
    n_blk = -(-S // BLK)
    pad = n_blk * BLK - S
    kb = jnp.pad(k, ((0, 0), (0, pad), (0, 0), (0, 0))).reshape(B, n_blk, BLK, H, hd).transpose(0, 3, 1, 2, 4)
    vb = jnp.pad(v, ((0, 0), (0, pad), (0, 0), (0, 0))).reshape(B, n_blk, BLK, H, hd).transpose(0, 3, 1, 2, 4)
    kmean = jnp.mean(kb.astype(jnp.float32), axis=3)
    k_eff = min(MOBA_TOPK, max(n_blk - 1, 1))
    scale = HEAD_DIM ** -0.5
    b_ix = jnp.arange(B)[:, None, None, None]
    h_ix = jnp.arange(H)[None, :, None, None]
    blk_ids = jnp.arange(n_blk)

    def step(c):
        qs = c * CH
        tq = qs + jnp.arange(CH)
        cur = qs // BLK
        qc = lax.dynamic_slice_in_dim(q, qs, CH, axis=1)
        gate = jnp.einsum('bqhd,bhnd->bhqn', qc.astype(jnp.float32), kmean)
        gate = jnp.where(blk_ids < cur, gate, -LARGE)
        _, sel = lax.top_k(gate, k_eff)
        valid = sel < cur
        kg = kb[b_ix, h_ix, sel].reshape(B, H, CH, k_eff * BLK, hd)
        vg = vb[b_ix, h_ix, sel].reshape(B, H, CH, k_eff * BLK, hd)
        msel = jnp.broadcast_to(valid[..., None], valid.shape + (BLK,)).reshape(B, H, CH, k_eff * BLK)
        k_own = lax.dynamic_index_in_dim(kb, cur, axis=2, keepdims=False)
        v_own = lax.dynamic_index_in_dim(vb, cur, axis=2, keepdims=False)
        own_pos = cur * BLK + jnp.arange(BLK)
        mown = jnp.broadcast_to(own_pos[None, :] <= tq[:, None], (B, H, CH, BLK))
        s_sel = jnp.einsum('bqhd,bhqkd->bhqk', qc, kg).astype(jnp.float32) * scale
        s_own = jnp.einsum('bqhd,bhkd->bhqk', qc, k_own).astype(jnp.float32) * scale
        p = masked_softmax(jnp.concatenate([s_sel, s_own], axis=-1), jnp.concatenate([msel, mown], axis=-1))
        p = p.astype(vg.dtype)
        o = (jnp.einsum('bhqk,bhqkd->bqhd', p[..., :k_eff * BLK], vg)
             + jnp.einsum('bhqk,bhkd->bqhd', p[..., k_eff * BLK:], v_own))
        return o.reshape(B, CH, D_MODEL).astype(h.dtype)

    out = lax.map(step, jnp.arange(S // CH))
    out = out.transpose(1, 0, 2, 3).reshape(B, S, D_MODEL)
    return out @ w_o

def swiglu(h, wg, wu, wd):
    return (jax.nn.silu(h @ wg) * (h @ wu)) @ wd

def setup_inputs(seed: int = 0) -> dict:
    key = jax.random.key(seed)
    ks = jax.random.split(key, 20)

    def nrm(k, shape, s):
        return jax.random.normal(k, shape, jnp.float32) * s

    x = nrm(ks[0], (BATCH, SEQ, D_MODEL), 1.0)
    positions = jnp.broadcast_to(jnp.arange(SEQ, dtype=jnp.int32)[None, :], (BATCH, SEQ))
    nsa_col = np.ones((NSA_IN,), np.float32)
    for m in (1, 3, 5):
        s0 = NSA_Q_DIM + m * NSA_KV_DIM
        nsa_col[s0:s0 + NSA_KV_DIM] = BETA
    nsa_w_in = nrm(ks[1], (N_NSA, D_MODEL, NSA_IN), D_MODEL ** -0.5) * jnp.asarray(nsa_col)
    nsa_w_o = nrm(ks[2], (N_NSA, NSA_Q_DIM, D_MODEL), BETA * NSA_Q_DIM ** -0.5)
    nsa_ck_pos = nrm(ks[3], (N_NSA, CMP_BLOCK, HEAD_DIM), 0.02)
    nsa_ck_w1 = nrm(ks[4], (N_NSA, CMP_BLOCK * HEAD_DIM, CMP_HIDDEN), (CMP_BLOCK * HEAD_DIM) ** -0.5)
    nsa_ck_w2 = nrm(ks[5], (N_NSA, CMP_HIDDEN, HEAD_DIM), CMP_HIDDEN ** -0.5)
    nsa_cv_pos = nrm(ks[6], (N_NSA, CMP_BLOCK, HEAD_DIM), 0.02)
    nsa_cv_w1 = nrm(ks[7], (N_NSA, CMP_BLOCK * HEAD_DIM, CMP_HIDDEN), (CMP_BLOCK * HEAD_DIM) ** -0.5)
    nsa_cv_w2 = nrm(ks[8], (N_NSA, CMP_HIDDEN, HEAD_DIM), CMP_HIDDEN ** -0.5)
    moba_col = np.ones((3 * D_MODEL,), np.float32)
    moba_col[2 * D_MODEL:] = BETA
    moba_w_in = nrm(ks[9], (N_MOBA, D_MODEL, 3 * D_MODEL), D_MODEL ** -0.5) * jnp.asarray(moba_col)
    moba_w_o = nrm(ks[10], (N_MOBA, D_MODEL, D_MODEL), BETA * D_MODEL ** -0.5)
    ffn_wg = nrm(ks[11], (DEPTH, D_MODEL, D_FF), D_MODEL ** -0.5)
    ffn_wu = nrm(ks[12], (DEPTH, D_MODEL, D_FF), D_MODEL ** -0.5)
    ffn_wd = nrm(ks[13], (DEPTH, D_FF, D_MODEL), BETA * D_FF ** -0.5)
    ln1_g = 1.0 + nrm(ks[14], (DEPTH, D_MODEL), 0.02)
    ln1_b = nrm(ks[15], (DEPTH, D_MODEL), 0.02)
    ln2_g = 1.0 + nrm(ks[16], (DEPTH, D_MODEL), 0.02)
    ln2_b = nrm(ks[17], (DEPTH, D_MODEL), 0.02)
    return {'x': x, 'positions': positions,
            'nsa_w_in': nsa_w_in, 'nsa_w_o': nsa_w_o,
            'nsa_ck_pos': nsa_ck_pos, 'nsa_ck_w1': nsa_ck_w1, 'nsa_ck_w2': nsa_ck_w2,
            'nsa_cv_pos': nsa_cv_pos, 'nsa_cv_w1': nsa_cv_w1, 'nsa_cv_w2': nsa_cv_w2,
            'moba_w_in': moba_w_in, 'moba_w_o': moba_w_o,
            'ffn_wg': ffn_wg, 'ffn_wu': ffn_wu, 'ffn_wd': ffn_wd,
            'ln1_g': ln1_g, 'ln1_b': ln1_b, 'ln2_g': ln2_g, 'ln2_b': ln2_b}

def reference(x, positions, nsa_w_in, nsa_w_o, nsa_ck_pos, nsa_ck_w1, nsa_ck_w2,
              nsa_cv_pos, nsa_cv_w1, nsa_cv_w2, moba_w_in, moba_w_o,
              ffn_wg, ffn_wu, ffn_wd, ln1_g, ln1_b, ln2_g, ln2_b):
    for i in range(DEPTH):
        j = i // 2
        if i % 2 == 0:
            a = nsa_mixer(x, positions, nsa_w_in[j], nsa_w_o[j], nsa_ck_pos[j], nsa_ck_w1[j],
                          nsa_ck_w2[j], nsa_cv_pos[j], nsa_cv_w1[j], nsa_cv_w2[j])
        else:
            a = moba_mixer(x, positions, moba_w_in[j], moba_w_o[j])
        x = layer_norm(ALPHA * x + a, ln1_g[i], ln1_b[i])
        f = swiglu(x, ffn_wg[i], ffn_wu[i], ffn_wd[i])
        x = layer_norm(ALPHA * x + f, ln2_g[i], ln2_b[i])
    return x


_drawn_inputs = setup_inputs


def setup_inputs(seed=0):
    import zlib

    import numpy as np

    out = dict(_drawn_inputs(seed))
    spreads = {}
    factors = {'nsa_ck_pos': 32.116, 'nsa_ck_w1': 5.706, 'nsa_ck_w2': 5.522, 'nsa_cv_pos': 28.62}
    for name, (base, spread) in spreads.items():
        noise = np.random.default_rng([zlib.crc32(name.encode()), seed]).standard_normal(out[name].shape)
        drawn = base * np.exp(spread * noise) if base else spread * noise
        out[name] = jnp.asarray(drawn.astype(out[name].dtype))
    for name, factor in factors.items():
        out[name] = (out[name] * factor).astype(out[name].dtype)
    return out
```

```python
import math
from contextlib import ExitStack

import numpy as np
import concourse.bass as bass
from concourse import mybir

S = 256
D = 1024
HD = 64
NH = 16
KV = 4
HALF = 2
P = 128
KT = D // P
FF = 2816
FC = 256
NFC = FF // FC
CB = 32
CS = 16
NCMP = (S - CB) // CS + 1
HID = 256
ROPE = HD // 4
THETA = 500000.0
ALPHA = (2 * 2) ** 0.25
EPS = 1e-5
SCALE = HD ** -0.5
NEG = -1e30
UNIT = 2048
SLOTS = 3
NSA_CHUNKS = 5
MOBA_CHUNKS = 6
U_NSA = 0
U_WO0 = U_NSA + 2 * NSA_CHUNKS
U_FF0 = U_WO0 + 4
U_MOBA = U_FF0 + 3 * NFC
U_WO1 = U_MOBA + 2 * MOBA_CHUNKS
U_FF1 = U_WO1 + 4
UNITS = U_FF1 + 3 * NFC
NSA_JOBS = 16
MOBA_JOBS = 8


def build(nc, x_rows, x_cols, stream, w_gates, w1, w2, cpos, positions, norms, out):
    f32 = mybir.dt.float32
    f32r = mybir.dt.float32r
    bf16 = mybir.dt.bfloat16
    i32 = mybir.dt.int32
    ALU = mybir.AluOpType
    ACT = mybir.ActivationFunctionType
    AX = mybir.AxisListType

    with ExitStack() as ctx:
        def sb(name, shape, dt=f32):
            return ctx.enter_context(nc.sbuf_tensor(name, shape, dt))

        def sem(name):
            return ctx.enter_context(nc.semaphore(name))

        raw = sb("raw", [P, SLOTS, UNIT])
        w_hi = sb("w_hi", [P, SLOTS, UNIT], f32r)
        w_lo = sb("w_lo", [P, SLOTS, UNIT], f32r)
        x = sb("x", [P, HALF, D])
        a_hi = sb("a_hi", [P, HALF, KT, P], f32r)
        a_lo = sb("a_lo", [P, HALF, KT, P], f32r)
        kz = sb("kz", [P, 8, 2, S])
        qT = sb("qT", [P, 8, S])
        rows = sb("rows", [P, 2, HALF, 512])
        twice = sb("twice", [P, HALF, 8, 2, HD])
        arena = sb("arena", [P, 4, 2048])
        values = arena[:, 0, :].rearrange("p (h n) -> p h n", h=HALF)
        o_rows = arena[:, 1, :].rearrange("p (h n) -> p h n", h=HALF)
        probs = arena[:, 2, 0:1536].rearrange("p (b n) -> p b n", b=2)
        probsT = arena[:, 3, 0:1536].rearrange("p (b n) -> p b n", b=2)
        w1_sb = arena[:, :, :].rearrange("p (a b) (j n) -> p a (b j) n", a=2, n=HID)
        gain = sb("gain", [P, 2, D])
        h_hi = sb("h_hi", [P, HALF, 2, P], f32r)
        h_lo = sb("h_lo", [P, HALF, 2, P], f32r)
        silu = arena[:, 2, 1536:2048].rearrange("p (h n) -> p h n", h=HALF)
        h_rows = arena[:, 3, 1536:2048].rearrange("p (h n) -> p h n", h=HALF)
        blocks = sb("blocks", [P, 2, CS, KV, NCMP])
        hidT = sb("hidT", [P, 2, 2, KV, 16])
        hid_rep = arena[:, 3, 1536:2048].rearrange("p (m b n) -> p m b n", m=2, b=2)
        w2k_sb = sb("w2k_sb", [P, 2, 2, HD])
        w2v_sb = sb("w2v_sb", [P, 2, HD])
        wg_raw = sb("wg_raw", [P, KT, 48])
        wg_hi = sb("wg_hi", [P, KT, 48], f32r)
        wg_lo = sb("wg_lo", [P, KT, 48], f32r)
        cpos_sb = sb("cpos_sb", [P, 2, CS])
        kcz = sb("kcz", [P, KV, 2, 16])
        vcz = sb("vcz", [P, 2, 8, HD])
        e_cmp = values[:, :, 512:768].rearrange("p h (n c) -> p h n c", c=16)
        e_cmpT = values[:, :, 768:1024].rearrange("p b (h r) -> p b h r", h=HALF)
        cmp_stat = sb("cmp_stat", [P, 4, HALF * NH])
        gates = sb("gates", [P, HALF, NH, 3])
        neg_max = sb("neg_max", [P, 12, HALF, 4])
        sums = sb("sums", [P, 12, HALF, 4])
        coef = sb("coef", [P, HALF, 4])
        o_part = arena[:, 2, 1536:2048].rearrange("p (h n d) -> p h n d", h=HALF, d=HD)
        pos_i = sb("pos_i", [P, HALF], i32)
        pos_f = sb("pos_f", [P, HALF])
        inv = sb("inv", [P, 16])
        phase = sb("phase", [P, 2, 16])
        ang = sb("ang", [P, 3, HALF, 16])
        cos2 = sb("cos2", [P, HALF, 16])
        sin2 = sb("sin2", [P, HALF, 16])
        turn = sb("turn", [P, 2, HALF, 8, 16])
        ident = sb("ident", [P, P])
        ident_b = sb("ident_b", [P, P], bf16)
        causal = sb("causal", [P, 2, P], bf16)
        cmp_mask = sb("cmp_mask", [P, HALF, 16])
        row_ok = sb("row_ok", [P, HALF])
        own_head = sb("own_head", [P, 8])
        bn = sb("bn", [P, 2, 6])
        mean_var = sb("mean_var", [P, 4, HALF, 2])
        var_eps = sb("var_eps", [P, 4, HALF])
        rstd = sb("rstd", [P, 4, HALF])
        minus_half = sb("minus_half", [P, 1])
        ps = ctx.enter_context(nc.psum_tensor("ps", [P, 8, 512], f32))

        raw_in = [sem(f"raw_in{s}") for s in range(SLOTS)]
        hi_ready = sem("hi_ready")
        lo_ready = sem("lo_ready")
        w_used = sem("w_used")
        xT_in = sem("xT_in")
        x_in = sem("x_in")
        small_in = sem("small_in")
        w1_in = sem("w1_in")
        gain_in = sem("gain_in")
        consts = sem("consts")
        a_hi_ready = sem("a_hi_ready")
        a_lo_ready = sem("a_lo_ready")
        wg_hi_ready = sem("wg_hi_ready")
        wg_lo_ready = sem("wg_lo_ready")
        evac = sem("evac")
        values_twice = sem("values_twice")
        roped = sem("roped")
        twice_ready = sem("twice_ready")
        turned = sem("turned")
        set_a = sem("set_a")
        set_v = sem("set_v")
        angles_ready = sem("angles_ready")
        sincos_ready = sem("sincos_ready")
        hid_done = sem("hid_done")
        hid_ready = sem("hid_ready")
        rep_ready = sem("rep_ready")
        kv_cmp_done = sem("kv_cmp_done")
        kv_cmp_ready = sem("kv_cmp_ready")
        gates_done = sem("gates_done")
        gates_ready = sem("gates_ready")
        s_cmp_done = sem("s_cmp_done")
        s_cmp_ready = sem("s_cmp_ready")
        e_cmp_ready = sem("e_cmp_ready")
        e_cmpT_done = sem("e_cmpT_done")
        e_cmpT_ready = sem("e_cmpT_ready")
        o_cmp_done = sem("o_cmp_done")
        o_cmp_used = sem("o_cmp_used")
        s_ready = sem("s_ready")
        max_ready = sem("max_ready")
        p_ready = sem("p_ready")
        pT_done = sem("pT_done")
        pT_ready = sem("pT_ready")
        pv_done = sem("pv_done")
        o_used = sem("o_used")
        o_ready = sem("o_ready")
        oT_done = sem("oT_done")
        silu_ready = sem("silu_ready")
        h_ready = sem("h_ready")
        hT_done = sem("hT_done")
        h_hi_ready = sem("h_hi_ready")
        h_lo_ready = sem("h_lo_ready")
        var_ready = sem("var_ready")
        rstd_ready = sem("rstd_ready")
        x_ready = sem("x_ready")
        xT_done = sem("xT_done")
        v_step = sem("v_step")
        g_step = sem("g_step")
        stored = sem("stored")

        block = ctx.enter_context(nc.Block())

        SMALL = 6
        A_X, A_O0, A_N0, A_N1, A_O1, A_N2 = 2, 6, 8, 10, 14, 16
        KC, VC, Q0, Q1, KS, KW, MQ0, MQ1, MK0, MK1 = range(10)

        def nsa_job(i):
            g, branch, j = i // 4, i // 2 % 2, i % 2
            return 2 * g + j, branch * KV + g, [branch * 256 + g * HD] * 2, i // 2, j

        def moba_job(i):
            return i, i, [(2 * i + h) * HD for h in range(2)], NSA_JOBS // 2 + i // 2, i % 2

        NSA = dict(jobs=NSA_JOBS, job=nsa_job, j0=0, t0=0, a0=A_X, ends=[3, 7, 11, 15])
        MOBA = dict(jobs=MOBA_JOBS, job=moba_job, j0=NSA_JOBS, t0=4, a0=A_N1, ends=[1, 3, 5, 7])

        acc_flat = ps[:, :, :].rearrange("p b n -> p (b n)")
        x_cols_raw = twice[:, :, :, :, :].rearrange("p h g t d -> p h (g t d)")
        set_ps = ps[:, 4:6, :].rearrange("p b (t r) -> p (b t) r", r=S)
        hT_ps = ps[:, 2, :].rearrange("p (h t r) -> p h t r", h=HALF, t=2)
        oT_ps = ps[:, 4, :].rearrange("p (h t r) -> p h t r", h=HALF, t=2)

        def set_target(k, lo, hi):
            if k in (Q0, Q1, MQ0, MQ1):
                i = k % 2 if k >= MQ0 else k - Q0
                return qT[lo:hi, 4 * i:4 * i + 4, :]
            i = (k - KS) if k < MQ0 else k - MK0
            return kz[lo:hi, 4 * i:4 * i + 4, lo // HD, :]

        @block.sync
        def _(sp):
            sp.dma_start(x_cols_raw, x_cols).then_inc(xT_in, 16)
            for s in range(SLOTS):
                sp.dma_start(raw[:, s, :], stream[s]).then_inc(raw_in[s], 16)
            with sp.Fori(1, UNITS // SLOTS) as t:
                for s in range(SLOTS):
                    sp.wait_ge(lo_ready, (t - 1) * SLOTS + s + 1)
                    unit = stream[bass.ds(t * SLOTS + s, 1), :, :].rearrange("a p n -> (a p) n")
                    sp.dma_start(raw[:, s, :], unit).then_inc(raw_in[s], 16)
            for half in range(HALF):
                sp.wait_ge(x_ready, 6 + half + 1)
                sp.dma_start(out[half], x[:, half, :]).then_inc(stored, 16)
            sp.wait_ge(stored, 16 * HALF)

        @block.gpsimd
        def _(gp):
            steps = [0]

            def link(ins):
                steps[0] += 1
                ins.then_inc(g_step, 1)
                gp.wait_ge(g_step, steps[0])

            freqs = np.power(np.float32(THETA), -np.arange(0, ROPE, 2, dtype=np.float32) / np.float32(ROPE))
            for j in range(ROPE // 2):
                nc.gpsimd.memset(inv[:, j:j + 1], float(freqs[j]))
                nc.gpsimd.memset(inv[:, 8 + j:9 + j], float(freqs[j]))
            nc.gpsimd.memset(phase[:, :, 0:8], 0.0)
            nc.gpsimd.memset(phase[:, 0, 8:16], 0.25)
            nc.gpsimd.memset(phase[:, 1, 8:16], math.pi / 2)
            nc.gpsimd.memset(minus_half[:, :], -0.5)
            nc.gpsimd.memset(row_ok[:, :], 1.0)
            nc.gpsimd.memset(own_head[:, :], 1.0)
            nc.gpsimd.memset(causal[:, :, :], 0.0)
            nc.gpsimd.memset(cmp_mask[:, :, :], 0.0)
            nc.gpsimd.memset(hidT[:, :, :, :, :], 0.0)
            nc.gpsimd.memset(kcz[:, :, :, :], 0.0)
            nc.gpsimd.memset(ident_b[:, :], 0.0)
            link(nc.gpsimd.memset(ident[:, :], 0.0))
            for m in (ident, ident_b):
                nc.gpsimd.affine_select(out=m[:, :], in_=m[:, :], compare_op=ALU.not_equal, fill=1.0, base=0,
                                        pattern=[[-1, P]], channel_multiplier=1)
            nc.gpsimd.affine_select(out=causal[:, :, :], in_=causal[:, :, :], compare_op=ALU.is_ge, fill=NEG,
                                    base=0, pattern=[[0, 2], [-1, P]], channel_multiplier=1)
            nc.gpsimd.affine_select(out=cmp_mask[:, :, :], in_=cmp_mask[:, :, :], compare_op=ALU.is_ge, fill=NEG,
                                    base=1 - CB, pattern=[[P, HALF], [-CS, 16]], channel_multiplier=1)
            nc.gpsimd.affine_select(out=row_ok[:, :], in_=row_ok[:, :], compare_op=ALU.is_ge, fill=0.0,
                                    base=1 - CB, pattern=[[P, HALF]], channel_multiplier=1)
            link(nc.gpsimd.affine_select(out=own_head[:, :], in_=own_head[:, :], compare_op=ALU.is_ge, fill=0.0,
                                         base=0, pattern=[[-16, 8]], channel_multiplier=1))
            nc.gpsimd.affine_select(out=own_head[:, :], in_=own_head[:, :], compare_op=ALU.is_ge, fill=0.0,
                                    base=15, pattern=[[16, 8]], channel_multiplier=-1).then_inc(consts, 1)
            nc.gpsimd.memset(kz[:, :, :, :], 0.0).then_inc(consts, 1)
            for l in range(4):
                if l > 0:
                    gp.wait_ge(x_ready, 2 * l)
                gp.dma_start(gain[:, 0, :], norms[l, 0:1, :].to_broadcast([P, D])).then_inc(gain_in, 16)
                gp.dma_start(gain[:, 1, :], norms[l, 1:2, :].to_broadcast([P, D])).then_inc(gain_in, 16)
                for half in range(HALF):
                    gp.wait_ge(var_ready, 2 * l + half + 1)
                    link(nc.gpsimd.tensor_scalar(var_eps[:, l, half:half + 1], mean_var[:, l, half, 1:2],
                                                 1.0, EPS, ALU.mult, ALU.add))
                    nc.gpsimd.tensor_tensor(rstd[:, l, half:half + 1], var_eps[:, l, half:half + 1],
                                            minus_half[:, :], ALU.pow).then_inc(rstd_ready, 1)

        @block.scalar
        def _(act):
            act.dma_start(pos_i[:, :], positions).then_inc(small_in, 16)
            act.dma_start(wg_raw[:, :, :], w_gates).then_inc(small_in, 16)
            act.dma_start(cpos_sb[:, :, :], cpos).then_inc(small_in, 16)
            act.dma_start(w2k_sb[:, :, 0, :], w2[:, 0, :, :]).then_inc(small_in, 16)
            act.dma_start(w2k_sb[:, :, 1, :], w2[:, 0, :, :]).then_inc(small_in, 16)
            act.dma_start(w2v_sb[:, :, :], w2[:, 1, :, :]).then_inc(small_in, 16)
            act.dma_start(w1_sb, w1).then_inc(w1_in, 16)
            act.dma_start(x[:, :, :], x_rows).then_inc(x_in, 16)
            units = [0]

            def copy(dst, src, scale=1.0):
                return nc.scalar.activation(dst, src, ACT.Copy, scale=scale)

            def round_unit(s, arrived, used):
                act.wait_ge(raw_in[s], arrived)
                if used is not None:
                    act.wait_ge(w_used, used)
                copy(w_hi[:, s, :], raw[:, s, :]).then_inc(hi_ready, 1)

            def round_to(end):
                for u in range(units[0], end):
                    round_unit(u % SLOTS, 16 * (u // SLOTS + 1), u - SLOTS + 1 if u >= SLOTS else None)
                units[0] = max(units[0], end)

            def keys_twice(b):
                for t in range(2):
                    last = copy(twice[:, :, 0:4, t, :],
                                rows[:, b, :, 0:256].rearrange("p h (g d) -> p h g d", g=KV))
                last.then_inc(twice_ready, 1)

            def copy_set(k):
                act.wait_ge(turned, k + 1)
                if k == Q0:
                    act.wait_ge(consts, 2)
                copy(set_target(k, 0, HD), set_ps[0:HD]).then_inc(set_a, 1)

            act.wait_ge(xT_in, 16)
            for half in range(HALF):
                copy(a_hi[:, half, :, :].rearrange("p k r -> p (k r)"), x_cols_raw[:, half, :]).then_inc(a_hi_ready, 1)
            round_to(1)
            act.wait_ge(angles_ready, 1)
            nc.scalar.activation(ang[:, 2], ang[:, 1], ACT.Sin).then_inc(sincos_ready, 1)
            round_to(3)
            act.wait_ge(small_in, 16 * SMALL)
            copy(wg_hi[:, :, :], wg_raw[:, :, :]).then_inc(wg_hi_ready, 1)
            round_to(4)

            act.wait_ge(w_used, 2)
            copy(rows[:, 0, :, :], ps[:, 0:2, :]).then_inc(evac, 1)
            round_to(5)
            act.wait_ge(evac, 1)
            act.wait_ge(a_lo_ready, A_X)
            for t in range(2):
                copy(twice[:, :, 4:8, t, :], rows[:, 0, :, 256:512].rearrange("p h (g d) -> p h g d", g=KV))
            act.wait_ge(roped, 1)
            keys_twice(0)
            round_to(6)
            act.wait_ge(w_used, 4)
            copy(rows[:, 1, :, :], ps[:, 2:4, :], SCALE).then_inc(evac, 1)
            round_to(8)
            act.wait_ge(w_used, 6)
            copy(rows[:, 0, :, :], ps[:, 0:2, :], SCALE).then_inc(evac, 1)
            round_to(9)
            copy_set(Q0)
            act.wait_ge(hid_done, 1)
            for kv in range(2):
                for m in range(2):
                    at = (2 * kv + m) * 64
                    last = nc.scalar.activation(hidT[:, kv, m, :, 0:NCMP],
                                                ps[:, 6, at:at + KV * NCMP].rearrange("p (g n) -> p g n", g=KV),
                                                ACT.Gelu_apprx_tanh)
            last.then_inc(hid_ready, 1)
            round_to(10)
            act.wait_ge(w_used, 8)
            copy(rows[:, 1, :, 0:256], ps[:, 2:4, 0:256])
            copy(values[:, :, 0:256], ps[:, 2:4, 256:512]).then_inc(evac, 1)
            copy_set(Q1)
            act.wait_ge(roped, 4)
            keys_twice(1)
            round_to(11)
            act.wait_ge(w_used, 10)
            copy(rows[:, 0, :, 0:256], ps[:, 0:2, 0:256])
            copy(values[:, :, 256:512], ps[:, 0:2, 256:512]).then_inc(evac, 1)
            round_to(12)
            act.wait_ge(gates_done, 1)
            nc.scalar.activation(gates[:, :, :, :].rearrange("p h n c -> p h (n c)"),
                                 ps[:, 6, 0:96].rearrange("p (h n) -> p h n", h=HALF),
                                 ACT.Sigmoid).then_inc(gates_ready, 1)
            copy_set(KS)
            act.wait_ge(roped, 5)
            keys_twice(0)
            round_to(13)
            act.wait_ge(s_cmp_ready, 1)
            nc.scalar.activation(e_cmp[:, :, :, :], e_cmp[:, :, :, :], ACT.Exp).then_inc(e_cmp_ready, 1)
            copy_set(KW)
            act.wait_ge(e_cmpT_done, 1)
            copy(e_cmpT, ps[:, 6, :].rearrange("p (b h r) -> p b h r", b=2, h=HALF)).then_inc(e_cmpT_ready, 1)

            def outputs_hi(g, t0):
                act.wait_ge(oT_done, t0 + g + 1)
                copy(a_hi[:, :, 2 * g:2 * g + 2, :], oT_ps).then_inc(a_hi_ready, 1)

            def attend(jobs, job, j0, t0, a0, ends):
                for i in range(jobs + 3):
                    if i < jobs:
                        _, _, _, grp, j = job(i)
                        b = i % 2
                        act.wait_ge(max_ready, j0 + i + 1)
                        if j0 + i >= 2:
                            act.wait_ge(pT_done, j0 + i - 1)
                        for half in range(HALF):
                            keys = P * (half + 1)
                            for h in range(2):
                                c = 2 * j + h
                                at = 2 * P * half + h * keys
                                last = nc.scalar.activation(probs[:, b, at:at + keys],
                                                            ps[:, 2 - 2 * half + b, h * keys:(h + 1) * keys], ACT.Exp,
                                                            bias=neg_max[:, grp, half, c:c + 1],
                                                            accum_out=sums[:, grp, half, c:c + 1])
                        last.then_inc(p_ready, 1)
                    if i - 3 in ends:
                        outputs_hi(ends.index(i - 3), t0)

            def norm_hi(l):
                for half in range(HALF):
                    act.wait_ge(xT_done, 2 * l + half + 1)
                    copy(a_hi[:, half, :, :].rearrange("p k r -> p (k r)"),
                         acc_flat[:, 1024 * half:1024 * (half + 1)]).then_inc(a_hi_ready, 1)

            def ffn(u0, c0):
                def silu_of(c, whole):
                    act.wait_ge(w_used, whole)
                    nc.scalar.activation(silu[:, :, :], ps[:, 0:2, 0:FC], ACT.Silu).then_inc(silu_ready, 1)

                def hidden_hi(c):
                    act.wait_ge(hT_done, c0 + c + 1)
                    copy(h_hi[:, :, :, :], hT_ps).then_inc(h_hi_ready, 1)

                def round_in(c, j):
                    round_unit((u0 + j) % SLOTS, ((u0 + j) // SLOTS + 1) * 16 + c * 16, 3 * c + (u0 + j - 2))

                silu_of(0, u0 + 2)
                round_to(u0 + 4)
                hidden_hi(0)
                round_to(u0 + 5)
                with act.Fori(1, NFC - 1) as c:
                    round_in(c, 2)
                    silu_of(c, 3 * c + (u0 + 1))
                    round_in(c, 3)
                    hidden_hi(c)
                    round_in(c, 4)
                units[0] = u0 + 3 * (NFC - 1) + 2
                c = NFC - 1
                round_to(u0 + 3 * c + 3)
                silu_of(c, u0 + 3 * c + 1)
                round_to(min(UNITS, u0 + 3 * c + 4))
                hidden_hi(c)
                round_to(min(UNITS, u0 + 3 * c + 5))

            attend(**NSA)
            round_to(U_FF0 + 2)
            round_to(U_FF0 + 3)
            norm_hi(0)
            ffn(U_FF0, 0)
            round_to(U_MOBA + 3)
            norm_hi(1)
            for n in range(MOBA_CHUNKS):
                round_to(min(U_MOBA + 2 * n + 4, U_WO1 + 3))
                act.wait_ge(w_used, U_MOBA + 2 * n + 2)
                b = n % 2
                if n in (2, 3):
                    act.wait_ge(turned, MQ0 + n - 1)
                if n < 4:
                    copy(rows[:, b, :, :], ps[:, 2 * b:2 * b + 2, :], SCALE if n < 2 else 1.0).then_inc(evac, 1)
                else:
                    copy(values[:, :, (n - 4) * 512:(n - 3) * 512], ps[:, 2 * b:2 * b + 2, :]).then_inc(evac, 1)
                round_to(min(U_MOBA + 2 * n + 5, U_WO1 + 3))
                if 2 <= n:
                    copy_set(MQ0 + n - 2)
            round_to(U_WO1 + 3)
            attend(**MOBA)
            round_to(U_FF1 + 3)
            norm_hi(2)
            ffn(U_FF1, NFC)

        @block.vector
        def _(dve):
            steps = [0]
            units = [0]

            def link(ins):
                steps[0] += 1
                ins.then_inc(v_step, 1)
                dve.wait_ge(v_step, steps[0])

            def minus(dst, a, b):
                return nc.vector.tensor_tensor(dst, a, b, ALU.subtract)

            def rest_of_unit(s, rounded):
                dve.wait_ge(hi_ready, rounded)
                minus(w_lo[:, s, :], raw[:, s, :], w_hi[:, s, :].bitcast(f32)).then_inc(lo_ready, 1)

            def rest_to(end):
                for u in range(units[0], end):
                    rest_of_unit(u % SLOTS, u + 1)
                units[0] = max(units[0], end)

            def rotate(b, count, heads):
                dve.wait_ge(evac, count)
                r = rows[:, b, :, 0:heads * HD].rearrange("p h (n d) -> p h n d", d=HD)
                t, u = turn[:, 0, :, 0:heads, :], turn[:, 1, :, 0:heads, :]

                def wide(table, lo, hi):
                    return table[:, :, lo:hi].unsqueeze(2).to_broadcast([P, HALF, heads, hi - lo])
                nc.vector.tensor_tensor(t, r[:, :, :, 0:16], wide(cos2, 0, 16), ALU.mult)
                nc.vector.tensor_tensor(u[:, :, :, 0:8], r[:, :, :, 8:16], wide(sin2, 0, 8), ALU.mult)
                link(nc.vector.tensor_tensor(u[:, :, :, 8:16], r[:, :, :, 0:8], wide(sin2, 8, 16), ALU.mult))
                nc.vector.tensor_tensor(r[:, :, :, 0:16], t, u, ALU.add).then_inc(roped, 1)
                dve.wait_ge(roped, count)

            def copy_set(k):
                dve.wait_ge(turned, k + 1)
                nc.vector.tensor_copy(set_target(k, HD, P), set_ps[HD:P]).then_inc(set_v, 1)

            for half in range(HALF):
                dve.wait_ge(a_hi_ready, half + 1)
                minus(a_lo[:, half, :, :].rearrange("p k r -> p (k r)"), x_cols_raw[:, half, :],
                      a_hi[:, half, :, :].rearrange("p k r -> p (k r)").bitcast(f32)).then_inc(a_lo_ready, 1)
            rest_to(1)
            dve.wait_ge(small_in, 16 * SMALL)
            dve.wait_ge(consts, 1)
            link(nc.vector.tensor_copy(pos_f[:, :], pos_i[:, :]))
            link(nc.vector.tensor_tensor(ang[:, 0], pos_f[:, :].unsqueeze(2).to_broadcast([P, HALF, 16]),
                                         inv[:, :].unsqueeze(1).to_broadcast([P, HALF, 16]), ALU.mult))
            link(nc.vector.scalar_tensor_tensor(ang[:, 1], ang[:, 0], 1.0 / (2 * math.pi),
                                                phase[:, 0:1, :].to_broadcast([P, HALF, 16]), ALU.mult, ALU.add))
            ROUND = 1.5 * 2.0 ** 23
            link(nc.vector.tensor_scalar(ang[:, 1], ang[:, 1], ROUND, None, ALU.add))
            link(nc.vector.tensor_scalar(ang[:, 1], ang[:, 1], ROUND, None, ALU.subtract))
            C1 = 6.28125
            C2 = float(np.floor((2 * math.pi - C1) * 2 ** 20) / 2 ** 20)
            C3 = 2 * math.pi - C1 - C2
            for part in (C1, C2, C3):
                link(nc.vector.scalar_tensor_tensor(ang[:, 0], ang[:, 1], -part, ang[:, 0], ALU.mult, ALU.add))
            link(nc.vector.tensor_tensor(ang[:, 0], ang[:, 0], phase[:, 1:2, :].to_broadcast([P, HALF, 16]), ALU.add))
            LIMIT = 3.1415925
            nc.vector.tensor_scalar(ang[:, 1], ang[:, 0], LIMIT, -LIMIT, ALU.min, ALU.max).then_inc(angles_ready, 1)
            rest_to(3)
            dve.wait_ge(wg_hi_ready, 1)
            minus(wg_lo[:, :, :], wg_raw[:, :, :], wg_hi[:, :, :].bitcast(f32)).then_inc(wg_lo_ready, 1)
            dve.wait_ge(sincos_ready, 1)
            nc.vector.tensor_copy(cos2[:, :, 0:8], ang[:, 2, :, 8:16])
            nc.vector.tensor_copy(cos2[:, :, 8:16], ang[:, 2, :, 8:16])
            nc.vector.tensor_scalar(sin2[:, :, 0:8], ang[:, 2, :, 0:8], -1.0, None, ALU.mult)
            link(nc.vector.tensor_copy(sin2[:, :, 8:16], ang[:, 2, :, 0:8]))
            rest_to(4)

            rotate(0, 1, KV)
            rest_to(5)
            for kv, k in ((0, KC), (1, VC)):
                dve.wait_ge(turned, k + 1)
                for part in range(2):
                    lo = HD * part
                    src = ps[lo:lo + HD, 4 + 2 * kv:6 + 2 * kv, :].rearrange("p b (g n j) -> p j (b g) n", n=16, j=CS)
                    last = nc.vector.tensor_tensor(
                        blocks[lo:lo + HD, kv, :, :, :], src[:, :, :, part:part + NCMP],
                        cpos_sb[lo:lo + HD, kv, :].unsqueeze(2).unsqueeze(3).to_broadcast([HD, CS, KV, NCMP]), ALU.add)
                last.then_inc(set_v, 1)
            rest_to(6)
            rotate(1, 2, 8)
            rest_to(8)
            rotate(0, 3, 8)
            copy_set(Q0)
            rest_to(9)
            dve.wait_ge(hid_ready, 1)
            for m in range(2):
                last = nc.vector.tensor_copy(
                    hid_rep[:, m, :, :].rearrange("p b (g r n) -> p (b g) r n", g=2, r=4),
                    hidT[:, 1, m, :, :].unsqueeze(2).to_broadcast([P, KV, 4, 16]))
            last.then_inc(rep_ready, 1)
            rest_to(10)
            rotate(1, 4, KV)
            copy_set(Q1)
            dve.wait_ge(kv_cmp_done, 1)
            for part in range(2):
                lo = HD * part
                nc.vector.tensor_copy(kcz[lo:lo + HD, :, part, :],
                                      ps[lo:lo + HD, 7, 0:64].rearrange("p (g n) -> p g n", g=KV))
            for hb in range(2):
                last = nc.vector.tensor_tensor(
                    vcz[:, hb, :, :], ps[:, 7, 64 * (hb + 1):64 * (hb + 2)].unsqueeze(1).to_broadcast([P, 8, HD]),
                    own_head[:, :].unsqueeze(2).to_broadcast([P, 8, HD]), ALU.mult)
            last.then_inc(kv_cmp_ready, 1)
            rest_to(11)
            rotate(0, 5, KV)
            rest_to(12)
            copy_set(KS)
            dve.wait_ge(s_cmp_done, 1)
            link(nc.vector.tensor_tensor(
                e_cmp[:, :, :, :], ps[:, 7, :].rearrange("p (h n c) -> p h n c", h=HALF, c=16),
                cmp_mask[:, :, :].unsqueeze(2).to_broadcast([P, HALF, NH, 16]), ALU.add))
            link(nc.vector.tensor_reduce(cmp_stat[:, 0, :].rearrange("p (h n) -> p h n", h=HALF), e_cmp, AX.X, ALU.max))
            minus(e_cmp, e_cmp, cmp_stat[:, 0, :].rearrange("p (h n) -> p h n", h=HALF).unsqueeze(3).to_broadcast([P, HALF, NH, 16])).then_inc(s_cmp_ready, 1)
            copy_set(KW)
            rest_to(13)
            dve.wait_ge(e_cmp_ready, 1)
            link(nc.vector.tensor_reduce(cmp_stat[:, 1, :].rearrange("p (h n) -> p h n", h=HALF), e_cmp, AX.X, ALU.add))
            link(nc.vector.reciprocal(cmp_stat[:, 2, :], cmp_stat[:, 1, :]))
            dve.wait_ge(gates_ready, 1)
            by_head = cmp_stat[:, 2:4, :].rearrange("p s (h n) -> p s h n", h=HALF)
            link(nc.vector.tensor_tensor(by_head[:, 1], by_head[:, 0], gates[:, :, :, 0], ALU.mult))
            link(nc.vector.tensor_tensor(by_head[:, 0], by_head[:, 1],
                                         row_ok[:, :].unsqueeze(2).to_broadcast([P, HALF, NH]), ALU.mult))
            dve.wait_ge(o_cmp_done, 1)
            link(nc.vector.tensor_tensor(
                o_rows.rearrange("p h (n d) -> p (h n) d", d=HD), acc_flat[:, 0:2048].rearrange("p (n d) -> p n d", d=HD),
                cmp_stat[:, 2, :].unsqueeze(2).to_broadcast([P, HALF * NH, HD]), ALU.mult))
            nc.vector.tensor_copy(coef[:, 0, 0:1], cmp_stat[:, 2, 0:1]).then_inc(o_cmp_used, 1)

            def row_maxima(job, j0, i):
                _, _, _, grp, j = job(i)
                b = i % 2
                dve.wait_ge(s_ready, j0 + i + 1)
                for half in range(HALF):
                    keys = P * (half + 1)
                    last = nc.vector.tensor_reduce(
                        neg_max[:, grp, half, 2 * j:2 * j + 2],
                        ps[:, 2 - 2 * half + b, 0:2 * keys].rearrange("p (h k) -> p h k", h=2), AX.X, ALU.max, negate=True)
                last.then_inc(max_ready, 1)

            def gather_group(grp, nsa):
                dve.wait_ge(pv_done, 2 * grp + 2)
                src = ps[:, 6 + grp % 2, :].rearrange("p (n d) -> p n d", d=HD)
                link(nc.vector.reciprocal(coef[:, :, :], sums[:, grp, :, :]))
                flat = coef[:, :, :].rearrange("p h n -> p (h n)").unsqueeze(2).to_broadcast([P, 8, HD])
                if nsa:
                    g, branch = grp // 2, grp % 2
                    link(nc.vector.tensor_tensor(coef[:, :, :], coef[:, :, :], gates[:, :, 4 * g:4 * g + 4, 1 + branch], ALU.mult))
                    nc.vector.tensor_tensor(o_part[:, :, :, :].rearrange("p h n d -> p (h n) d"), src, flat, ALU.mult).then_inc(o_used, 1)
                    dve.wait_ge(o_used, grp + 1)
                    dst = o_rows[:, :, 256 * g:256 * g + 256]
                    ins = nc.vector.tensor_tensor(dst, dst, o_part[:, :, :, :].rearrange("p h n d -> p h (n d)"), ALU.add)
                    if branch == 1:
                        ins.then_inc(o_ready, 1)
                        dve.wait_ge(o_ready, g + 1)
                    else:
                        link(ins)
                else:
                    g = grp - NSA_JOBS // 2
                    dst = o_rows[:, :, 256 * g:256 * g + 256].rearrange("p h (n d) -> p h n d", d=HD)
                    nc.vector.tensor_tensor(dst, src.rearrange("p (h n) d -> p h n d", h=HALF),
                                            coef[:, :, :].unsqueeze(3).to_broadcast([P, HALF, 4, HD]),
                                            ALU.mult).then_inc(o_used, 1)
                    dve.wait_ge(o_used, grp + 1)

            def attend(jobs, job, j0, t0, a0, ends):
                for i in range(jobs + 3):
                    if i < jobs:
                        row_maxima(job, j0, i)
                    if 1 <= i <= jobs:
                        dve.wait_ge(pT_done, j0 + i)
                        if j0 + i >= 3:
                            dve.wait_ge(pv_done, j0 + i - 2)
                        nc.vector.tensor_copy(probsT[:, (i - 1) % 2, :], acc_flat[:, 2048:2048 + 768]).then_inc(pT_ready, 1)
                    if i >= 3 and i % 2 == 1:
                        gather_group((j0 + i - 3) // 2, j0 == 0)
                    if i - 3 in ends:
                        g = ends.index(i - 3)
                        dve.wait_ge(a_hi_ready, a0 + g + 1)
                        minus(a_lo[:, :, 2 * g:2 * g + 2, :], oT_ps,
                              a_hi[:, :, 2 * g:2 * g + 2, :].bitcast(f32)).then_inc(a_lo_ready, 1)

            def norm(l, whole, a0):
                dve.wait_ge(w_used, whole)
                dve.wait_ge(gain_in, 32 * (l + 1))
                if l == 0:
                    dve.wait_ge(x_in, 16)

                def add_residual(half):
                    link(nc.vector.scalar_tensor_tensor(x[:, half, :], x[:, half, :], ALPHA,
                                                        acc_flat[:, 2048 + 1024 * half:3072 + 1024 * half], ALU.mult, ALU.add))

                def statistics(half):
                    for part in range(2):
                        last = nc.vector.bn_stats(bn[:, part, :], x[:, half, 512 * part:512 * (part + 1)])
                    link(last)
                    nc.vector.bn_aggr(mean_var[:, l, half, :], bn[:, :, :].rearrange("p a b -> p (a b)")).then_inc(var_ready, 1)
                    dve.wait_ge(var_ready, 2 * l + half + 1)

                def finish(half):
                    dve.wait_ge(rstd_ready, 2 * l + half + 1)
                    link(nc.vector.tensor_scalar(x[:, half, :], x[:, half, :], mean_var[:, l, half, 0:1],
                                                 rstd[:, l, half:half + 1], ALU.subtract, ALU.mult))
                    link(nc.vector.tensor_tensor(x[:, half, :], x[:, half, :], gain[:, 0, :], ALU.mult))
                    nc.vector.tensor_tensor(x[:, half, :], x[:, half, :], gain[:, 1, :], ALU.add).then_inc(x_ready, 1)

                def columns_lo(half):
                    dve.wait_ge(a_hi_ready, a0 + half + 1)
                    minus(a_lo[:, half, :, :].rearrange("p k r -> p (k r)"), acc_flat[:, 1024 * half:1024 * (half + 1)],
                          a_hi[:, half, :, :].rearrange("p k r -> p (k r)").bitcast(f32)).then_inc(a_lo_ready, 1)

                add_residual(0)
                statistics(0)
                add_residual(1)
                finish(0)
                statistics(1)
                if l < 3:
                    columns_lo(0)
                finish(1)
                if l < 3:
                    columns_lo(1)

            def ffn(u0, c0):
                def hidden(c):
                    dve.wait_ge(silu_ready, c0 + c + 1)
                    nc.vector.tensor_tensor(h_rows[:, :, :], silu[:, :, :], ps[:, 0:2, FC:2 * FC],
                                            ALU.mult).then_inc(h_ready, 1)

                def hidden_lo(c):
                    dve.wait_ge(h_hi_ready, c0 + c + 1)
                    minus(h_lo[:, :, :, :], hT_ps, h_hi[:, :, :, :].bitcast(f32)).then_inc(h_lo_ready, 1)

                def rest_in(c, j):
                    rest_of_unit((u0 + j) % SLOTS, 3 * c + (u0 + j + 1))

                hidden(0)
                rest_to(u0 + 4)
                hidden_lo(0)
                rest_to(u0 + 5)
                with dve.Fori(1, NFC - 1) as c:
                    rest_in(c, 2)
                    hidden(c)
                    rest_in(c, 3)
                    hidden_lo(c)
                    rest_in(c, 4)
                units[0] = u0 + 3 * (NFC - 1) + 2
                c = NFC - 1
                rest_to(u0 + 3 * c + 3)
                hidden(c)
                rest_to(min(UNITS, u0 + 3 * c + 4))
                hidden_lo(c)
                rest_to(min(UNITS, u0 + 3 * c + 5))

            attend(**NSA)
            rest_to(U_FF0 + 2)
            norm(0, U_FF0, A_O0)
            rest_to(U_FF0 + 3)
            ffn(U_FF0, 0)
            norm(1, U_MOBA, A_N0)
            rest_to(U_MOBA + 3)
            for n in range(MOBA_CHUNKS):
                rest_to(min(U_MOBA + 2 * n + 4, U_WO1 + 3))
                if n < 4:
                    rotate(n % 2, NSA_CHUNKS + n + 1, 8)
                rest_to(min(U_MOBA + 2 * n + 5, U_WO1 + 3))
                if 2 <= n:
                    copy_set(MQ0 + n - 2)
            rest_to(U_WO1 + 3)
            attend(**MOBA)
            rest_to(U_FF1 + 2)
            norm(2, U_FF1, A_O1)
            rest_to(U_FF1 + 3)
            ffn(U_FF1, NFC)
            norm(3, UNITS, None)

        @block.tensor
        def _(pe):
            def product(dst, hi, lo, m_hi, m_lo, start, stop):
                nc.tensor.matmul(dst, hi, m_hi, start=start, stop=False)
                nc.tensor.matmul(dst, hi, m_lo, start=False, stop=False)
                return nc.tensor.matmul(dst, lo, m_hi, start=False, stop=stop)

            def rows_by_weights(u, unit, half, bank):
                s = u % SLOTS
                for k in range(4):
                    at = slice(512 * k, 512 * (k + 1))
                    kt = 4 * unit + k
                    last = product(ps[:, bank, :], a_hi[:, half, kt, :], a_lo[:, half, kt, :],
                                   w_hi[:, s, at], w_lo[:, s, at], start=kt == 0, stop=kt == KT - 1)
                return last

            def chunk(u, banks, count=None, last_use=True):
                for unit in range(2):
                    pe.wait_ge(lo_ready, (u if count is None else count) + unit + 1)
                    for half in range(HALF):
                        last = rows_by_weights(u + unit, unit, half, banks[half])
                    last.then_inc(w_used, 1)

            def first_chunk(u, ready, l):
                for half in range(HALF):
                    if l is not None:
                        pe.wait_ge(x_ready, 2 * l + half + 1)
                        for k in range(KT):
                            last = nc.tensor.transpose(acc_flat[:, 1024 * half + P * k:1024 * half + P * (k + 1)],
                                                       x[:, half, P * k:P * (k + 1)], ident[:, :])
                        last.then_inc(xT_done, 1)
                    pe.wait_ge(a_lo_ready, ready + half + 1)
                    for unit in range(2):
                        pe.wait_ge(lo_ready, u + unit + 1)
                        last = rows_by_weights(u + unit, unit, half, half)
                        if half == 1:
                            last.then_inc(w_used, 1)

            def set_free(k):
                if k > Q0:
                    pe.wait_ge(set_a, k - 2)
                pe.wait_ge(set_v, k)

            def turn_rows(k, b):
                for t in range(4):
                    for half in range(HALF):
                        last = nc.tensor.transpose(set_ps[:, t, P * half:P * (half + 1)],
                                                   rows[:, b, half, P * t:P * (t + 1)], ident[:, :])
                last.then_inc(turned, 1)

            def turn_twice(g0, dst):
                for g in range(KV):
                    for half in range(HALF):
                        last = nc.tensor.transpose(dst[:, g, P * half:P * (half + 1)],
                                                   twice[:, half, g0 + g, :, :].rearrange("p t d -> p (t d)"), ident[:, :])
                last.then_inc(turned, 1)

            first_chunk(0, 0, None)
            chunk(2, (2, 3))
            pe.wait_ge(consts, 1)
            pe.wait_ge(twice_ready, 1)
            turn_twice(0, set_ps)
            turn_twice(4, ps[:, 6:8, :].rearrange("p b (t r) -> p (b t) r", r=S))
            pe.wait_ge(evac, 1)
            chunk(4, (0, 1))
            pe.wait_ge(roped, 2)
            set_free(Q0)
            turn_rows(Q0, 1)
            pe.wait_ge(w1_in, 16)
            for kv in range(2):
                for m in range(2):
                    at = (2 * kv + m) * 64
                    for j in range(CS):
                        last = nc.tensor.matmul(ps[:, 6, at:at + KV * NCMP], w1_sb[:, kv, j, P * m:P * (m + 1)],
                                                blocks[:, kv, j, :, :].rearrange("p g n -> p (g n)"),
                                                start=j == 0, stop=j == CS - 1)
            last.then_inc(hid_done, 1)
            pe.wait_ge(evac, 2)
            chunk(6, (2, 3))
            pe.wait_ge(roped, 3)
            set_free(Q1)
            turn_rows(Q1, 0)
            pe.wait_ge(rep_ready, 1)
            for m in range(2):
                nc.tensor.matmul(ps[:, 7, 0:64], w2k_sb[:, m, :, :].rearrange("p t d -> p (t d)"),
                                 hidT[:, 0, m, :, :].rearrange("p g n -> p (g n)"), start=m == 0, stop=m == 1)
            for hb in range(2):
                for m in range(2):
                    last = nc.tensor.matmul(ps[:, 7, 64 * (hb + 1):64 * (hb + 2)], hid_rep[:, m, hb, :], w2v_sb[:, m, :],
                                            start=m == 0, stop=m == 1)
            last.then_inc(kv_cmp_done, 1)
            pe.wait_ge(evac, 3)
            chunk(8, (0, 1))
            pe.wait_ge(wg_lo_ready, 1)
            for half in range(HALF):
                for k in range(KT):
                    last = product(ps[:, 6, 48 * half:48 * (half + 1)], a_hi[:, half, k, :], a_lo[:, half, k, :],
                                   wg_hi[:, k, :], wg_lo[:, k, :], start=k == 0, stop=k == KT - 1)
            last.then_inc(gates_done, 1)
            pe.wait_ge(twice_ready, 2)
            set_free(KS)
            turn_twice(0, set_ps)
            pe.wait_ge(kv_cmp_ready, 1)
            for half in range(HALF):
                for t in range(8):
                    at = 256 * half + 32 * t
                    last = nc.tensor.matmul(ps[:, 7, at:at + 32], qT[:, t, P * half:P * (half + 1)],
                                            kcz[:, t // 2, :, :].rearrange("p t n -> p (t n)"), start=True, stop=True)
            last.then_inc(s_cmp_done, 1)
            pe.wait_ge(twice_ready, 3)
            set_free(KW)
            turn_twice(0, set_ps)
            pe.wait_ge(gates_ready, 1)
            pe.wait_ge(e_cmp_ready, 1)
            for hb in range(2):
                for half in range(HALF):
                    at = P * (2 * hb + half)
                    last = nc.tensor.transpose(ps[:, 6, at:at + P],
                                               e_cmp[:, half, 8 * hb:8 * hb + 8, :].rearrange("p n c -> p (n c)"), ident[:, :])
            last.then_inc(e_cmpT_done, 1)
            pe.wait_ge(evac, 5)
            pe.wait_ge(e_cmpT_ready, 1)
            for half in range(HALF):
                for hb in range(2):
                    last = nc.tensor.matmul(ps[:, 2 * half + hb, :], e_cmpT[:, hb, half, :],
                                            vcz[:, hb, :, :].rearrange("p n d -> p (n d)"), start=True, stop=True)
            last.then_inc(o_cmp_done, 1)
            pe.wait_ge(o_cmp_used, 1)
            set_free(MQ0)

            def scores(job, j0, i):
                q, k, _, _, _ = job(i)
                b = i % 2
                if j0 + i >= 2:
                    pe.wait_ge(p_ready, j0 + i - 1)
                for half in range(HALF):
                    keys = P * (half + 1)
                    dst = ps[:, 2 - 2 * half + b, 0:2 * keys]
                    nc.tensor.matmul(dst, qT[:, q, P * half:P * (half + 1)], kz[:, k, :, 0:keys],
                                     start=True, stop=False)
                    last = nc.tensor.matmul(dst.rearrange("p (h k) -> p h k", h=2)[:, :, keys - P:keys],
                                            ident_b[:, :], causal[:, :, :], start=False, stop=True)
                last.then_inc(s_ready, 1)

            def turn_probs(i_all, outputs):
                b = i_all % 2
                pe.wait_ge(p_ready, i_all + 1)
                if i_all >= 1:
                    pe.wait_ge(pT_ready, i_all)
                pe.wait_ge(a_lo_ready, outputs)
                for h in range(2):
                    for half in range(HALF):
                        at = 256 * half + h * P * (half + 1)
                        nc.tensor.transpose(acc_flat[:, 2048 + P * (2 * h + half):2048 + P * (2 * h + half + 1)],
                                            probs[:, b, at:at + P], ident[:, :])
                for h in range(2):
                    at = 256 + h * S + P
                    last = nc.tensor.transpose(acc_flat[:, 2560 + P * h:2560 + P * (h + 1)], probs[:, b, at:at + P], ident[:, :])
                last.then_inc(pT_done, 1)

            def weigh_values(job, j0, i):
                _, _, cols, grp, j = job(i)
                b = i % 2
                pe.wait_ge(pT_ready, j0 + i + 1)
                if grp >= 2:
                    pe.wait_ge(o_used, grp - 1)
                bank = 6 + grp % 2
                for h in range(2):
                    for half in range(HALF):
                        at = 256 * half + HD * (2 * j + h)
                        dst = ps[:, bank, at:at + HD]
                        c = slice(cols[h], cols[h] + HD)
                        last = nc.tensor.matmul(dst, probsT[:, b, P * (2 * h + half):P * (2 * h + half + 1)],
                                                values[:, 0, c], start=True, stop=half == 0)
                        if half == 1:
                            last = nc.tensor.matmul(dst, probsT[:, b, 512 + P * h:512 + P * (h + 1)], values[:, 1, c],
                                                    start=False, stop=True)
                last.then_inc(pv_done, 1)

            def turn_outputs(g, t0):
                if t0 == 0:
                    pe.wait_ge(o_ready, g + 1)
                else:
                    pe.wait_ge(o_used, NSA_JOBS // 2 + g + 1)
                for half in range(HALF):
                    for t in range(2):
                        last = nc.tensor.transpose(oT_ps[:, half, t, :],
                                                   o_rows[:, half, 256 * g + P * t:256 * g + P * (t + 1)], ident[:, :])
                last.then_inc(oT_done, 1)

            def attend(jobs, job, j0, t0, a0, ends):
                scores(job, j0, 0)
                scores(job, j0, 1)
                done = a0
                for i in range(jobs + 2):
                    if i < jobs:
                        turn_probs(j0 + i, done)
                        if i + 2 < jobs:
                            scores(job, j0, i + 2)
                        weigh_values(job, j0, i)
                    if i - 2 in ends:
                        if i >= jobs and done > a0:
                            pe.wait_ge(a_lo_ready, done)
                        turn_outputs(ends.index(i - 2), t0)
                        done += 1

            def output_weights(u, ready):
                pe.wait_ge(a_lo_ready, ready)
                chunk(u, (4, 6))
                chunk(u + 2, (5, 7))

            def ffn(u0, c0, ready, l):
                def down(s, start, stop):
                    for k in range(2):
                        for half in range(HALF):
                            for part in range(3):
                                for c in range(2):
                                    at = slice(1024 * k + 512 * c, 1024 * k + 512 * (c + 1))
                                    last = nc.tensor.matmul(
                                        ps[:, 4 + 2 * half + c, :], (h_hi, h_hi, h_lo)[part][:, half, k, :],
                                        (w_hi, w_lo, w_hi)[part][:, s, at],
                                        start=start and k == 0 and part == 0, stop=stop and k == 1 and part == 2)
                    last.then_inc(w_used, 1)

                def turn_hidden(c):
                    pe.wait_ge(h_ready, c0 + c + 1)
                    for half in range(HALF):
                        for t in range(2):
                            last = nc.tensor.transpose(hT_ps[:, half, t, :], h_rows[:, half, P * t:P * (t + 1)], ident[:, :])
                    last.then_inc(hT_done, 1)

                def step(c, start=False):
                    chunk(u0 + 2, (0, 1), count=3 * c + (u0 - 1))
                    pe.wait_ge(h_lo_ready, c0 + c)
                    pe.wait_ge(lo_ready, 3 * c + (u0 + 2))
                    down((u0 + 1) % SLOTS, start, False)
                    turn_hidden(c)

                first_chunk(u0, ready, l)
                turn_hidden(0)
                step(1, start=True)
                with pe.Fori(2, NFC) as c:
                    step(c)
                pe.wait_ge(h_lo_ready, c0 + NFC)
                pe.wait_ge(lo_ready, u0 + 3 * NFC)
                down((u0 + 3 * NFC - 1) % SLOTS, False, True)

            attend(**NSA)
            output_weights(U_WO0, A_O0)
            ffn(U_FF0, 0, A_O0, 0)
            for n in range(MOBA_CHUNKS):
                if n == 0:
                    first_chunk(U_MOBA, A_N0, 1)
                else:
                    if n >= 2:
                        pe.wait_ge(evac, NSA_CHUNKS + n - 1)
                    b = 2 * (n % 2)
                    chunk(U_MOBA + 2 * n, (b, b + 1))
                if 1 <= n < 5:
                    pe.wait_ge(roped, NSA_CHUNKS + n)
                    set_free(MQ0 + n - 1)
                    turn_rows(MQ0 + n - 1, (n - 1) % 2)
            pe.wait_ge(evac, NSA_CHUNKS + MOBA_CHUNKS)
            set_free(MK1 + 1)
            attend(**MOBA)
            output_weights(U_WO1, A_O1)
            ffn(U_FF1, NFC, A_O1, 2)


def _unit(block):
    return block.reshape(-1, P, block.shape[-1]).transpose(1, 0, 2).reshape(P, -1)


def _columns(w, lo, hi):
    return [_unit(w[512 * i:512 * (i + 1), lo:hi]) for i in range(2)]


def _network(wg, wu, wd):
    units = []
    for c in range(NFC):
        at = slice(FC * c, FC * (c + 1))
        units += _columns(np.concatenate([wg[:, at], wu[:, at]], axis=1), 0, 2 * FC)
        if c > 0:
            units.append(_unit(wd[FC * (c - 1):FC * c]))
    units.append(_unit(wd[FC * (NFC - 1):]))
    return units


def kernel(x, positions, nsa_w_in, nsa_w_o, nsa_ck_pos, nsa_ck_w1, nsa_ck_w2, nsa_cv_pos, nsa_cv_w1, nsa_cv_w2,
           moba_w_in, moba_w_o, ffn_wg, ffn_wu, ffn_wd, ln1_g, ln1_b, ln2_g, ln2_b):
    import concourse.bacc as bacc
    from concourse.bass_utils import run_bass_kernel_spmd

    a = {k: np.asarray(v) for k, v in locals().items() if k not in ("bacc", "run_bass_kernel_spmd")}
    w_in, w_moba = a["nsa_w_in"][0], a["moba_w_in"][0]
    kv = NH * HD
    starts = [kv, 0, 512, kv + 512, kv + 1024]
    units = [u for c in starts for u in _columns(w_in, c, c + 512)]
    for c in range(2):
        units += _columns(a["nsa_w_o"][0], 512 * c, 512 * (c + 1))
    units += _network(a["ffn_wg"][0], a["ffn_wu"][0], a["ffn_wd"][0])
    for c in range(MOBA_CHUNKS):
        units += _columns(w_moba, 512 * c, 512 * (c + 1))
    for c in range(2):
        units += _columns(a["moba_w_o"][0], 512 * c, 512 * (c + 1))
    units += _network(a["ffn_wg"][1], a["ffn_wu"][1], a["ffn_wd"][1])

    def halves(w):
        return w.reshape(2, CS, HD, -1).transpose(0, 2, 1, 3).reshape(P, CS, -1)

    rows = a["x"][0].reshape(HALF, P, D)
    arrays = {
        "x_rows": rows.transpose(1, 0, 2),
        "x_cols": rows.reshape(HALF, P, KT, P).transpose(3, 0, 2, 1).reshape(P, HALF, KT * P),
        "stream": np.stack(units),
        "w_gates": w_in[:, kv + 6 * KV * HD:].reshape(KT, P, 3 * NH).transpose(1, 0, 2),
        "w1": np.stack([halves(a["nsa_ck_w1"][0]), halves(a["nsa_cv_w1"][0])], axis=1),
        "w2": np.stack([a[n][0].reshape(2, P, HD).transpose(1, 0, 2) for n in ("nsa_ck_w2", "nsa_cv_w2")], axis=1),
        "cpos": np.stack([a[n][0].reshape(2, CS, HD).transpose(0, 2, 1).reshape(P, CS)
                          for n in ("nsa_ck_pos", "nsa_cv_pos")], axis=1),
        "positions": a["positions"][0].reshape(HALF, P).transpose(1, 0),
        "norms": np.stack([np.stack([a[f"ln{i}_{p}"][l] for p in "gb"]) for l in range(2) for i in (1, 2)]),
    }
    nc = bacc.Bacc("TRN2", target_bir_lowering=False, num_devices=1)
    ins = {}
    for name, value in arrays.items():
        arrays[name] = np.ascontiguousarray(value)
        ins[name] = nc.dram_tensor(name, arrays[name].shape, mybir.dt.from_np(arrays[name].dtype),
                                   kind="ExternalInput").ap()
    out = nc.dram_tensor("out", [HALF, P, D], mybir.dt.float32, kind="ExternalOutput").ap()
    build(nc, ins["x_rows"], ins["x_cols"], ins["stream"], ins["w_gates"],
          ins["w1"], ins["w2"], ins["cpos"], ins["positions"], ins["norms"], out)
    result = run_bass_kernel_spmd(nc, [arrays], core_ids=[0])
    return result.results[0]["out"].reshape(1, S, D)
```

```python
import math
from contextlib import ExitStack

import numpy as np
import concourse.bass as bass
from concourse import mybir

S = 256
D = 1024
HD = 64
NH = 16
KV = 4
HALF = 2
P = 128
KT = D // P
FF = 2816
FC = 256
NFC = FF // FC
CB = 32
CS = 16
NCMP = (S - CB) // CS + 1
HID = 256
ROPE = HD // 4
THETA = 500000.0
ALPHA = (2 * 2) ** 0.25
EPS = 1e-5
SCALE = HD ** -0.5
NEG = -1e30
UNIT = 2048
SLOTS = 3
NSA_CHUNKS = 5
MOBA_CHUNKS = 6
U_NSA = 0
U_WO0 = U_NSA + 2 * NSA_CHUNKS
U_FF0 = U_WO0 + 4
U_MOBA = U_FF0 + 3 * NFC
U_WO1 = U_MOBA + 2 * MOBA_CHUNKS
U_FF1 = U_WO1 + 4
UNITS = U_FF1 + 3 * NFC
NSA_JOBS = 16
MOBA_JOBS = 8


def build(nc, x_rows, x_cols, stream, w_gates, w1, w2, cpos, positions, norms, out):
    f32 = mybir.dt.float32
    f32r = mybir.dt.float32r
    bf16 = mybir.dt.bfloat16
    i32 = mybir.dt.int32
    ALU = mybir.AluOpType
    ACT = mybir.ActivationFunctionType
    AX = mybir.AxisListType

    with ExitStack() as ctx:
        def sb(name, shape, dt=f32):
            return ctx.enter_context(nc.sbuf_tensor(name, shape, dt))

        def sem(name):
            return ctx.enter_context(nc.semaphore(name))

        raw = sb("raw", [P, SLOTS, UNIT])
        w_hi = sb("w_hi", [P, SLOTS, UNIT], f32r)
        w_lo = sb("w_lo", [P, SLOTS, UNIT], f32r)
        x = sb("x", [P, HALF, D])
        a_hi = sb("a_hi", [P, HALF, KT, P], f32r)
        a_lo = sb("a_lo", [P, HALF, KT, P], f32r)
        kz = sb("kz", [P, 8, 2, S])
        qT = sb("qT", [P, 8, S])
        rows = sb("rows", [P, 2, HALF, 512])
        twice = sb("twice", [P, HALF, 8, 2, HD])
        arena = sb("arena", [P, 4, 2048])
        values = arena[:, 0, :].rearrange("p (h n) -> p h n", h=HALF)
        o_rows = arena[:, 1, :].rearrange("p (h n) -> p h n", h=HALF)
        probs = arena[:, 2, 0:1536].rearrange("p (b n) -> p b n", b=2)
        probsT = arena[:, 3, 0:1536].rearrange("p (b n) -> p b n", b=2)
        w1_sb = arena[:, :, :].rearrange("p (a b) (j n) -> p a (b j) n", a=2, n=HID)
        gain = sb("gain", [P, 2, D])
        h_hi = sb("h_hi", [P, HALF, 2, P], f32r)
        h_lo = sb("h_lo", [P, HALF, 2, P], f32r)
        silu = arena[:, 2, 1536:2048].rearrange("p (h n) -> p h n", h=HALF)
        h_rows = arena[:, 3, 1536:2048].rearrange("p (h n) -> p h n", h=HALF)
        blocks = sb("blocks", [P, 2, CS, KV, NCMP])
        hidT = sb("hidT", [P, 2, 2, KV, 16])
        hid_rep = arena[:, 3, 1536:2048].rearrange("p (m b n) -> p m b n", m=2, b=2)
        w2k_sb = sb("w2k_sb", [P, 2, 2, HD])
        w2v_sb = sb("w2v_sb", [P, 2, HD])
        wg_raw = sb("wg_raw", [P, KT, 48])
        wg_hi = sb("wg_hi", [P, KT, 48], f32r)
        wg_lo = sb("wg_lo", [P, KT, 48], f32r)
        cpos_sb = sb("cpos_sb", [P, 2, CS])
        kcz = sb("kcz", [P, KV, 2, 16])
        vcz = sb("vcz", [P, 2, 8, HD])
        e_cmp = values[:, :, 512:768].rearrange("p h (n c) -> p h n c", c=16)
        e_cmpT = values[:, :, 768:1024].rearrange("p b (h r) -> p b h r", h=HALF)
        cmp_stat = sb("cmp_stat", [P, 4, HALF * NH])
        gates = sb("gates", [P, HALF, NH, 3])
        neg_max = sb("neg_max", [P, 12, HALF, 4])
        sums = sb("sums", [P, 12, HALF, 4])
        coef = sb("coef", [P, HALF, 4])
        o_part = arena[:, 2, 1536:2048].rearrange("p (h n d) -> p h n d", h=HALF, d=HD)
        pos_i = sb("pos_i", [P, HALF], i32)
        pos_f = sb("pos_f", [P, HALF])
        inv = sb("inv", [P, 16])
        phase = sb("phase", [P, 2, 16])
        ang = sb("ang", [P, 3, HALF, 16])
        cos2 = sb("cos2", [P, HALF, 16])
        sin2 = sb("sin2", [P, HALF, 16])
        turn = sb("turn", [P, 2, HALF, 8, 16])
        ident = sb("ident", [P, P])
        ident_b = sb("ident_b", [P, P], bf16)
        causal = sb("causal", [P, 2, P], bf16)
        cmp_mask = sb("cmp_mask", [P, HALF, 16])
        row_ok = sb("row_ok", [P, HALF])
        own_head = sb("own_head", [P, 8])
        bn = sb("bn", [P, 2, 6])
        mean_var = sb("mean_var", [P, 4, HALF, 2])
        var_eps = sb("var_eps", [P, 4, HALF])
        rstd = sb("rstd", [P, 4, HALF])
        minus_half = sb("minus_half", [P, 1])
        ps = ctx.enter_context(nc.psum_tensor("ps", [P, 8, 512], f32))

        raw_in = [sem(f"raw_in{s}") for s in range(SLOTS)]
        hi_ready = sem("hi_ready")
        lo_ready = sem("lo_ready")
        w_used = sem("w_used")
        xT_in = [sem(f"xT_in{h}") for h in range(HALF)]
        x_in = sem("x_in")
        small_in = sem("small_in")
        w1_in = sem("w1_in")
        gain_in = sem("gain_in")
        consts = sem("consts")
        a_hi_ready = sem("a_hi_ready")
        a_lo_ready = sem("a_lo_ready")
        wg_hi_ready = sem("wg_hi_ready")
        wg_lo_ready = sem("wg_lo_ready")
        evac = sem("evac")
        roped = sem("roped")
        twice_ready = sem("twice_ready")
        turned = sem("turned")
        set_a = sem("set_a")
        set_v = sem("set_v")
        angles_ready = sem("angles_ready")
        sincos_ready = sem("sincos_ready")
        hid_done = sem("hid_done")
        hid_ready = sem("hid_ready")
        rep_ready = sem("rep_ready")
        kv_cmp_done = sem("kv_cmp_done")
        kv_cmp_ready = sem("kv_cmp_ready")
        gates_done = sem("gates_done")
        gates_ready = sem("gates_ready")
        s_cmp_done = sem("s_cmp_done")
        s_cmp_ready = sem("s_cmp_ready")
        e_cmp_ready = sem("e_cmp_ready")
        e_cmpT_done = sem("e_cmpT_done")
        e_cmpT_ready = sem("e_cmpT_ready")
        o_cmp_done = sem("o_cmp_done")
        o_cmp_used = sem("o_cmp_used")
        s_ready = sem("s_ready")
        max_ready = sem("max_ready")
        p_ready = sem("p_ready")
        pT_done = sem("pT_done")
        pT_ready_a = sem("pT_ready_a")
        pT_ready_v = sem("pT_ready_v")
        pv_done = sem("pv_done")
        o_used = sem("o_used")
        o_ready = sem("o_ready")
        oT_done = sem("oT_done")
        silu_ready = sem("silu_ready")
        h_ready = sem("h_ready")
        hT_done = sem("hT_done")
        h_hi_ready = sem("h_hi_ready")
        h_lo_ready = sem("h_lo_ready")
        half_sums = sem("half_sums")
        var_ready = sem("var_ready")
        rstd_ready = sem("rstd_ready")
        x_ready = sem("x_ready")
        xT_done = sem("xT_done")
        v_step = sem("v_step")
        g_step = sem("g_step")
        stored = sem("stored")

        block = ctx.enter_context(nc.Block())

        SMALL = 6
        A_X, A_O0, A_N0, A_N1, A_O1 = 2, 6, 10, 14, 18
        KC, VC, Q0, Q1, KS, KW, MQ0, MQ1, MK0, MK1 = range(10)

        def nsa_job(i):
            g, branch, j = i // 4, i // 2 % 2, i % 2
            return 2 * g + j, branch * KV + g, [branch * 256 + g * HD] * 2, i // 2, j

        def moba_job(i):
            return i, i, [(2 * i + h) * HD for h in range(2)], NSA_JOBS // 2 + i // 2, i % 2

        NSA = dict(jobs=NSA_JOBS, job=nsa_job, j0=0, t0=0, a0=A_X)
        MOBA = dict(jobs=MOBA_JOBS, job=moba_job, j0=NSA_JOBS, t0=4, a0=A_N1)

        MOBA_BANKS = [0, 2, 0, 2, 0, 6]

        acc_flat = ps[:, :, :].rearrange("p b n -> p (b n)")
        x_cols_raw = twice[:, :, :, :, :].rearrange("p h g t d -> p h (g t d)")
        set_ps = ps[:, 4:6, :].rearrange("p b (t r) -> p (b t) r", r=S)
        hT_ps = ps[:, 2, :].rearrange("p (h t r) -> p h t r", h=HALF, t=2)

        def oT_ps(g):
            return ps[:, (0, 2, 1, 3)[g], :].rearrange("p (h t r) -> p h t r", h=HALF, t=2)

        win_ps = ps[:, 2:4, :].rearrange("p b (t r) -> p (b t) r", r=S)

        def set_target(k, lo, hi):
            if k in (Q0, Q1, MQ0, MQ1):
                i = k % 2 if k >= MQ0 else k - Q0
                return qT[lo:hi, 4 * i:4 * i + 4, :]
            i = (k - KS) if k < MQ0 else k - MK0
            return kz[lo:hi, 4 * i:4 * i + 4, lo // HD, :]

        @block.sync
        def _(sp):
            sp.dma_start(x_cols_raw[:, 0, :], x_cols[:, 0, :]).then_inc(xT_in[0], 16)
            for s in range(SLOTS):
                sp.dma_start(raw[:, s, :], stream[s]).then_inc(raw_in[s], 16)
                if s == 1:
                    sp.dma_start(x_cols_raw[:, 1, :], x_cols[:, 1, :]).then_inc(xT_in[1], 16)
            with sp.Fori(1, UNITS // SLOTS) as t:
                for s in range(SLOTS):
                    sp.wait_ge(lo_ready, (t - 1) * SLOTS + s + 1)
                    unit = stream[bass.ds(t * SLOTS + s, 1), :, :].rearrange("a p n -> (a p) n")
                    sp.dma_start(raw[:, s, :], unit).then_inc(raw_in[s], 16)
            for part in range(4):
                sp.wait_ge(x_ready, 12 + part + 1)
                half, at = part // 2, slice(512 * (part % 2), 512 * (part % 2 + 1))
                sp.dma_start(out[half, :, at], x[:, half, at]).then_inc(stored, 16)
            sp.wait_ge(stored, 16 * 4)

        @block.gpsimd
        def _(gp):
            steps = [0]

            def link(ins):
                steps[0] += 1
                ins.then_inc(g_step, 1)
                gp.wait_ge(g_step, steps[0])

            freqs = np.power(np.float32(THETA), -np.arange(0, ROPE, 2, dtype=np.float32) / np.float32(ROPE))
            for j in range(ROPE // 2):
                nc.gpsimd.memset(inv[:, j:j + 1], float(freqs[j]))
                nc.gpsimd.memset(inv[:, 8 + j:9 + j], float(freqs[j]))
            nc.gpsimd.memset(phase[:, :, 0:8], 0.0)
            nc.gpsimd.memset(phase[:, 0, 8:16], 0.25)
            nc.gpsimd.memset(phase[:, 1, 8:16], math.pi / 2)
            nc.gpsimd.memset(minus_half[:, :], -0.5)
            nc.gpsimd.memset(row_ok[:, :], 1.0)
            nc.gpsimd.memset(own_head[:, :], 1.0)
            nc.gpsimd.memset(causal[:, :, :], 0.0)
            nc.gpsimd.memset(cmp_mask[:, :, :], 0.0)
            nc.gpsimd.memset(hidT[:, :, :, :, :], 0.0)
            nc.gpsimd.memset(kcz[:, :, :, :], 0.0)
            nc.gpsimd.memset(ident_b[:, :], 0.0)
            link(nc.gpsimd.memset(ident[:, :], 0.0))
            for m in (ident, ident_b):
                nc.gpsimd.affine_select(out=m[:, :], in_=m[:, :], compare_op=ALU.not_equal, fill=1.0, base=0,
                                        pattern=[[-1, P]], channel_multiplier=1)
            nc.gpsimd.affine_select(out=causal[:, :, :], in_=causal[:, :, :], compare_op=ALU.is_ge, fill=NEG,
                                    base=0, pattern=[[0, 2], [-1, P]], channel_multiplier=1)
            nc.gpsimd.affine_select(out=cmp_mask[:, :, :], in_=cmp_mask[:, :, :], compare_op=ALU.is_ge, fill=NEG,
                                    base=1 - CB, pattern=[[P, HALF], [-CS, 16]], channel_multiplier=1)
            nc.gpsimd.affine_select(out=row_ok[:, :], in_=row_ok[:, :], compare_op=ALU.is_ge, fill=0.0,
                                    base=1 - CB, pattern=[[P, HALF]], channel_multiplier=1)
            link(nc.gpsimd.affine_select(out=own_head[:, :], in_=own_head[:, :], compare_op=ALU.is_ge, fill=0.0,
                                         base=0, pattern=[[-16, 8]], channel_multiplier=1))
            nc.gpsimd.affine_select(out=own_head[:, :], in_=own_head[:, :], compare_op=ALU.is_ge, fill=0.0,
                                    base=15, pattern=[[16, 8]], channel_multiplier=-1).then_inc(consts, 1)
            nc.gpsimd.memset(kz[:, :, :, :], 0.0).then_inc(consts, 1)
            for l in range(4):
                if l > 0:
                    gp.wait_ge(x_ready, 4 * l)
                gp.dma_start(gain[:, 0, :], norms[l, 0:1, :].to_broadcast([P, D])).then_inc(gain_in, 16)
                gp.dma_start(gain[:, 1, :], norms[l, 1:2, :].to_broadcast([P, D])).then_inc(gain_in, 16)
                for half in range(HALF):
                    gp.wait_ge(var_ready, 2 * l + half + 1)
                    link(nc.gpsimd.tensor_scalar(var_eps[:, l, half:half + 1], mean_var[:, l, half, 1:2],
                                                 1.0, EPS, ALU.mult, ALU.add))
                    nc.gpsimd.tensor_tensor(rstd[:, l, half:half + 1], var_eps[:, l, half:half + 1],
                                            minus_half[:, :], ALU.pow).then_inc(rstd_ready, 1)

        @block.scalar
        def _(act):
            act.dma_start(pos_i[:, :], positions).then_inc(small_in, 16)
            act.dma_start(wg_raw[:, :, :], w_gates).then_inc(small_in, 16)
            act.dma_start(cpos_sb[:, :, :], cpos).then_inc(small_in, 16)
            act.dma_start(w2k_sb[:, :, 0, :], w2[:, 0, :, :]).then_inc(small_in, 16)
            act.dma_start(w2k_sb[:, :, 1, :], w2[:, 0, :, :]).then_inc(small_in, 16)
            act.dma_start(w2v_sb[:, :, :], w2[:, 1, :, :]).then_inc(small_in, 16)
            units = [0]

            def copy(dst, src, scale=1.0):
                return nc.scalar.activation(dst, src, ACT.Copy, scale=scale)

            def round_unit(s, arrived, used):
                act.wait_ge(raw_in[s], arrived)
                if used is not None:
                    act.wait_ge(w_used, used)
                copy(w_hi[:, s, :], raw[:, s, :]).then_inc(hi_ready, 1)

            def round_to(end):
                for u in range(units[0], end):
                    round_unit(u % SLOTS, 16 * (u // SLOTS + 1), u - SLOTS + 1 if u >= SLOTS else None)
                units[0] = max(units[0], end)

            def write_twice(b, lo, hi):
                for t in range(2):
                    last = copy(twice[:, :, lo:hi, t, :],
                                rows[:, b, :, HD * lo:HD * hi].rearrange("p h (g d) -> p h g d", d=HD))
                return last

            def copy_set(k):
                act.wait_ge(turned, k + 1)
                if k == Q0:
                    act.wait_ge(consts, 2)
                copy(set_target(k, 0, HD), (win_ps if k == KW else set_ps)[0:HD]).then_inc(set_a, 1)

            def x_hi(half):
                act.wait_ge(xT_in[half], 16)
                copy(a_hi[:, half, :, :].rearrange("p k r -> p (k r)"), x_cols_raw[:, half, :]).then_inc(a_hi_ready, 1)

            x_hi(0)
            round_to(2)
            x_hi(1)
            act.wait_ge(angles_ready, 1)
            nc.scalar.activation(ang[:, 2], ang[:, 1], ACT.Sin).then_inc(sincos_ready, 1)
            round_to(3)
            for kv in range(2):
                act.dma_start(w1_sb[:, kv], w1[:, kv]).then_inc(w1_in, 16)
            act.wait_ge(small_in, 16 * SMALL)
            copy(wg_hi[:, :, :], wg_raw[:, :, :]).then_inc(wg_hi_ready, 1)
            round_to(4)

            act.wait_ge(w_used, 2)
            copy(rows[:, 0, :, :], ps[:, 0:2, :]).then_inc(evac, 1)
            round_to(5)
            act.wait_ge(evac, 1)
            act.wait_ge(a_lo_ready, A_X)
            write_twice(0, 4, 8)
            act.wait_ge(roped, 1)
            write_twice(0, 0, 4).then_inc(twice_ready, 1)
            round_to(6)
            act.wait_ge(w_used, 4)
            copy(rows[:, 1, :, :], ps[:, 2:4, :], SCALE).then_inc(evac, 1)
            round_to(8)
            act.wait_ge(w_used, 6)
            copy(rows[:, 0, :, :], ps[:, 0:2, :], SCALE).then_inc(evac, 1)
            copy_set(Q0)
            round_to(9)
            act.wait_ge(hid_done, 1)
            for kv in range(2):
                for m in range(2):
                    at = (2 * kv + m) * 64
                    last = nc.scalar.activation(hidT[:, kv, m, :, 0:NCMP],
                                                ps[:, 6, at:at + KV * NCMP].rearrange("p (g n) -> p g n", g=KV),
                                                ACT.Gelu_apprx_tanh)
            last.then_inc(hid_ready, 1)
            round_to(10)
            act.wait_ge(w_used, 8)
            copy(rows[:, 1, :, :], ps[:, 2:4, :]).then_inc(evac, 1)
            copy_set(Q1)
            act.wait_ge(roped, 4)
            write_twice(1, 0, 8).then_inc(twice_ready, 1)
            act.wait_ge(gates_done, 1)
            nc.scalar.activation(gates[:, :, :, :].rearrange("p h n c -> p h (n c)"),
                                 ps[:, 6, 0:96].rearrange("p (h n) -> p h n", h=HALF),
                                 ACT.Sigmoid).then_inc(gates_ready, 1)
            round_to(11)
            act.wait_ge(s_cmp_ready, 1)
            nc.scalar.activation(e_cmp[:, :, :, :], e_cmp[:, :, :, :], ACT.Exp).then_inc(e_cmp_ready, 1)
            round_to(12)
            act.wait_ge(w_used, 10)
            copy(values[:, :, 0:512], ps[:, 0:2, :]).then_inc(evac, 1)
            act.wait_ge(e_cmpT_done, 1)
            copy(e_cmpT, ps[:, 6, :].rearrange("p (b h r) -> p b h r", b=2, h=HALF)).then_inc(e_cmpT_ready, 1)
            copy_set(KS)
            copy_set(KW)
            act.dma_start(x[:, :, :], x_rows).then_inc(x_in, 16)

            def attend(jobs, job, j0, t0, a0):
                for i in range(jobs + 1):
                    if i < jobs:
                        _, _, _, grp, j = job(i)
                        b = i % 2
                        act.wait_ge(max_ready, j0 + i + 1)
                        if j0 + i >= 2:
                            act.wait_ge(pT_done, j0 + i - 1)
                        for half in range(HALF):
                            keys = P * (half + 1)
                            for h in range(2):
                                c = 2 * j + h
                                at = 2 * P * half + h * keys
                                last = nc.scalar.activation(probs[:, b, at:at + keys],
                                                            ps[:, 2 - 2 * half + b, h * keys:(h + 1) * keys], ACT.Exp,
                                                            bias=neg_max[:, grp, half, c:c + 1],
                                                            accum_out=sums[:, grp, half, c:c + 1])
                        last.then_inc(p_ready, 1)
                    if i >= 1:
                        act.wait_ge(pT_done, j0 + i)
                        if j0 + i >= 3:
                            act.wait_ge(pv_done, j0 + i - 2)
                        copy(probsT[:, (i - 1) % 2, 0:512], ps[:, 4, :]).then_inc(pT_ready_a, 1)
                for g in range(4):
                    act.wait_ge(oT_done, t0 + g + 1)
                    copy(a_hi[:, :, 2 * g:2 * g + 2, :], oT_ps(g)).then_inc(a_hi_ready, 1)

            def norm_hi(l):
                for half in range(HALF):
                    for part in range(2):
                        act.wait_ge(xT_done, 4 * l + 2 * half + part + 1)
                        copy(a_hi[:, half, 4 * part:4 * part + 4, :],
                             ps[:, 2 * half + part, :].rearrange("p (k r) -> p k r", k=4)).then_inc(a_hi_ready, 1)

            def ffn(u0, c0):
                def silu_of(c, whole):
                    act.wait_ge(w_used, whole)
                    nc.scalar.activation(silu[:, :, :], ps[:, 0:2, 0:FC], ACT.Silu).then_inc(silu_ready, 1)

                def hidden_hi(c):
                    act.wait_ge(hT_done, c0 + c + 1)
                    copy(h_hi[:, :, :, :], hT_ps).then_inc(h_hi_ready, 1)

                def round_in(c, j):
                    round_unit((u0 + j) % SLOTS, ((u0 + j) // SLOTS + 1) * 16 + c * 16, 3 * c + (u0 + j - 2))

                silu_of(0, u0 + 2)
                round_to(u0 + 4)
                hidden_hi(0)
                round_to(u0 + 5)
                with act.Fori(1, NFC - 1) as c:
                    round_in(c, 2)
                    silu_of(c, 3 * c + (u0 + 1))
                    round_in(c, 3)
                    hidden_hi(c)
                    round_in(c, 4)
                units[0] = u0 + 3 * (NFC - 1) + 2
                c = NFC - 1
                round_to(u0 + 3 * c + 3)
                silu_of(c, u0 + 3 * c + 1)
                round_to(min(UNITS, u0 + 3 * c + 4))
                hidden_hi(c)
                round_to(min(UNITS, u0 + 3 * c + 5))

            round_to(U_WO0 + 3)
            attend(**NSA)
            round_to(U_FF0 + 3)
            norm_hi(0)
            ffn(U_FF0, 0)
            round_to(U_MOBA + 3)
            norm_hi(1)
            for n in range(MOBA_CHUNKS):
                if 2 <= n:
                    copy_set(MQ0 + n - 2)
                round_to(min(U_MOBA + 2 * n + 4, U_WO1 + 3))
                act.wait_ge(w_used, U_MOBA + 2 * n + 2)
                b = n % 2
                if n in (2, 3):
                    act.wait_ge(turned, MQ0 + n - 1)
                if n < 4:
                    copy(rows[:, b, :, :], ps[:, 2 * b:2 * b + 2, :], SCALE if n < 2 else 1.0).then_inc(evac, 1)
                else:
                    bank = MOBA_BANKS[n]
                    copy(values[:, :, (n - 4) * 512:(n - 3) * 512], ps[:, bank:bank + 2, :]).then_inc(evac, 1)
                round_to(min(U_MOBA + 2 * n + 5, U_WO1 + 3))
            round_to(U_WO1 + 3)
            attend(**MOBA)
            round_to(U_FF1 + 3)
            norm_hi(2)
            ffn(U_FF1, NFC)

        @block.vector
        def _(dve):
            steps = [0]
            units = [0]

            def link(ins):
                steps[0] += 1
                ins.then_inc(v_step, 1)
                dve.wait_ge(v_step, steps[0])

            def step(ins):
                steps[0] += 1
                ins.then_inc(v_step, 1)
                return steps[0]

            def minus(dst, a, b):
                return nc.vector.tensor_tensor(dst, a, b, ALU.subtract)

            def rest_of_unit(s, rounded):
                dve.wait_ge(hi_ready, rounded)
                minus(w_lo[:, s, :], raw[:, s, :], w_hi[:, s, :].bitcast(f32)).then_inc(lo_ready, 1)

            def rest_to(end):
                for u in range(units[0], end):
                    rest_of_unit(u % SLOTS, u + 1)
                units[0] = max(units[0], end)

            def rotate(b, chunks, count, heads):
                dve.wait_ge(evac, chunks)
                r = rows[:, b, :, 0:heads * HD].rearrange("p h (n d) -> p h n d", d=HD)
                t, u = turn[:, 0, :, 0:heads, :], turn[:, 1, :, 0:heads, :]

                def wide(table, lo, hi):
                    return table[:, :, lo:hi].unsqueeze(2).to_broadcast([P, HALF, heads, hi - lo])
                nc.vector.tensor_tensor(t, r[:, :, :, 0:16], wide(cos2, 0, 16), ALU.mult)
                nc.vector.tensor_tensor(u[:, :, :, 0:8], r[:, :, :, 8:16], wide(sin2, 0, 8), ALU.mult)
                link(nc.vector.tensor_tensor(u[:, :, :, 8:16], r[:, :, :, 0:8], wide(sin2, 8, 16), ALU.mult))
                nc.vector.tensor_tensor(r[:, :, :, 0:16], t, u, ALU.add).then_inc(roped, 1)
                dve.wait_ge(roped, count)

            def copy_set(k):
                dve.wait_ge(turned, k + 1)
                nc.vector.tensor_copy(set_target(k, HD, P), (win_ps if k == KW else set_ps)[HD:P]).then_inc(set_v, 1)

            def x_lo(half):
                dve.wait_ge(a_hi_ready, half + 1)
                minus(a_lo[:, half, :, :].rearrange("p k r -> p (k r)"), x_cols_raw[:, half, :],
                      a_hi[:, half, :, :].rearrange("p k r -> p (k r)").bitcast(f32)).then_inc(a_lo_ready, 1)

            x_lo(0)
            rest_to(2)
            x_lo(1)
            dve.wait_ge(small_in, 16 * SMALL)
            dve.wait_ge(consts, 1)
            link(nc.vector.tensor_copy(pos_f[:, :], pos_i[:, :]))
            link(nc.vector.tensor_tensor(ang[:, 0], pos_f[:, :].unsqueeze(2).to_broadcast([P, HALF, 16]),
                                         inv[:, :].unsqueeze(1).to_broadcast([P, HALF, 16]), ALU.mult))
            link(nc.vector.scalar_tensor_tensor(ang[:, 1], ang[:, 0], 1.0 / (2 * math.pi),
                                                phase[:, 0:1, :].to_broadcast([P, HALF, 16]), ALU.mult, ALU.add))
            ROUND = 1.5 * 2.0 ** 23
            link(nc.vector.tensor_scalar(ang[:, 1], ang[:, 1], ROUND, None, ALU.add))
            link(nc.vector.tensor_scalar(ang[:, 1], ang[:, 1], ROUND, None, ALU.subtract))
            C1 = 6.28125
            C2 = float(np.floor((2 * math.pi - C1) * 2 ** 20) / 2 ** 20)
            C3 = 2 * math.pi - C1 - C2
            for part in (C1, C2, C3):
                link(nc.vector.scalar_tensor_tensor(ang[:, 0], ang[:, 1], -part, ang[:, 0], ALU.mult, ALU.add))
            link(nc.vector.tensor_tensor(ang[:, 0], ang[:, 0], phase[:, 1:2, :].to_broadcast([P, HALF, 16]), ALU.add))
            LIMIT = 3.1415925
            nc.vector.tensor_scalar(ang[:, 1], ang[:, 0], LIMIT, -LIMIT, ALU.min, ALU.max).then_inc(angles_ready, 1)
            rest_to(3)
            dve.wait_ge(wg_hi_ready, 1)
            minus(wg_lo[:, :, :], wg_raw[:, :, :], wg_hi[:, :, :].bitcast(f32)).then_inc(wg_lo_ready, 1)
            dve.wait_ge(sincos_ready, 1)
            nc.vector.tensor_copy(cos2[:, :, 0:8], ang[:, 2, :, 8:16])
            nc.vector.tensor_copy(cos2[:, :, 8:16], ang[:, 2, :, 8:16])
            nc.vector.tensor_scalar(sin2[:, :, 0:8], ang[:, 2, :, 0:8], -1.0, None, ALU.mult)
            link(nc.vector.tensor_copy(sin2[:, :, 8:16], ang[:, 2, :, 0:8]))
            rest_to(4)

            rotate(0, 1, 1, KV)
            rest_to(6)
            rotate(1, 2, 2, 8)
            for kv, k in ((0, KC), (1, VC)):
                dve.wait_ge(turned, k + 1)
                for part in range(2):
                    lo = HD * part
                    src = ps[lo:lo + HD, 4 + 2 * kv:6 + 2 * kv, :].rearrange("p b (g n j) -> p j (b g) n", n=16, j=CS)
                    last = nc.vector.tensor_tensor(
                        blocks[lo:lo + HD, kv, :, :, :], src[:, :, :, part:part + NCMP],
                        cpos_sb[lo:lo + HD, kv, :].unsqueeze(2).unsqueeze(3).to_broadcast([HD, CS, KV, NCMP]), ALU.add)
                last.then_inc(set_v, 1)
            rest_to(8)
            rotate(0, 3, 3, 8)
            copy_set(Q0)
            rest_to(9)
            dve.wait_ge(hid_ready, 1)
            for m in range(2):
                last = nc.vector.tensor_copy(
                    hid_rep[:, m, :, :].rearrange("p b (g r n) -> p (b g) r n", g=2, r=4),
                    hidT[:, 1, m, :, :].unsqueeze(2).to_broadcast([P, KV, 4, 16]))
            last.then_inc(rep_ready, 1)
            rest_to(10)
            rotate(1, 4, 4, 8)
            copy_set(Q1)
            dve.wait_ge(kv_cmp_done, 1)
            for part in range(2):
                lo = HD * part
                nc.vector.tensor_copy(kcz[lo:lo + HD, :, part, :],
                                      ps[lo:lo + HD, 7, 0:64].rearrange("p (g n) -> p g n", g=KV))
            for hb in range(2):
                last = nc.vector.tensor_tensor(
                    vcz[:, hb, :, :], ps[:, 7, 64 * (hb + 1):64 * (hb + 2)].unsqueeze(1).to_broadcast([P, 8, HD]),
                    own_head[:, :].unsqueeze(2).to_broadcast([P, 8, HD]), ALU.mult)
            last.then_inc(kv_cmp_ready, 1)
            dve.wait_ge(s_cmp_done, 1)
            link(nc.vector.tensor_tensor(
                e_cmp[:, :, :, :], ps[:, 7, :].rearrange("p (h n c) -> p h n c", h=HALF, c=16),
                cmp_mask[:, :, :].unsqueeze(2).to_broadcast([P, HALF, NH, 16]), ALU.add))
            link(nc.vector.tensor_reduce(cmp_stat[:, 0, :].rearrange("p (h n) -> p h n", h=HALF), e_cmp, AX.X, ALU.max))
            minus(e_cmp, e_cmp, cmp_stat[:, 0, :].rearrange("p (h n) -> p h n", h=HALF).unsqueeze(3).to_broadcast([P, HALF, NH, 16])).then_inc(s_cmp_ready, 1)
            rest_to(11)
            dve.wait_ge(e_cmp_ready, 1)
            link(nc.vector.tensor_reduce(cmp_stat[:, 1, :].rearrange("p (h n) -> p h n", h=HALF), e_cmp, AX.X, ALU.add))
            link(nc.vector.reciprocal(cmp_stat[:, 2, :], cmp_stat[:, 1, :]))
            dve.wait_ge(gates_ready, 1)
            by_head = cmp_stat[:, 2:4, :].rearrange("p s (h n) -> p s h n", h=HALF)
            link(nc.vector.tensor_tensor(by_head[:, 1], by_head[:, 0], gates[:, :, :, 0], ALU.mult))
            link(nc.vector.tensor_tensor(by_head[:, 0], by_head[:, 1],
                                         row_ok[:, :].unsqueeze(2).to_broadcast([P, HALF, NH]), ALU.mult))
            rest_to(12)
            copy_set(KS)
            copy_set(KW)
            dve.wait_ge(o_cmp_done, 1)
            nc.vector.tensor_tensor(
                o_rows.rearrange("p h (n d) -> p (h n) d", d=HD), acc_flat[:, 2048:4096].rearrange("p (n d) -> p n d", d=HD),
                cmp_stat[:, 2, :].unsqueeze(2).to_broadcast([P, HALF * NH, HD]), ALU.mult).then_inc(o_cmp_used, 1)
            rest_to(13)
            dve.wait_ge(o_cmp_used, 1)

            def row_maxima(job, j0, i):
                _, _, _, grp, j = job(i)
                b = i % 2
                dve.wait_ge(s_ready, j0 + i + 1)
                for half in range(HALF):
                    keys = P * (half + 1)
                    last = nc.vector.tensor_reduce(
                        neg_max[:, grp, half, 2 * j:2 * j + 2],
                        ps[:, 2 - 2 * half + b, 0:2 * keys].rearrange("p (h k) -> p h k", h=2), AX.X, ALU.max, negate=True)
                last.then_inc(max_ready, 1)

            def gather_group(grp, nsa):
                dve.wait_ge(pv_done, 2 * grp + 2)
                src = ps[:, 6 + grp % 2, :].rearrange("p (n d) -> p n d", d=HD)
                link(nc.vector.reciprocal(coef[:, :, :], sums[:, grp, :, :]))
                flat = coef[:, :, :].rearrange("p h n -> p (h n)").unsqueeze(2).to_broadcast([P, 8, HD])
                if nsa:
                    g, branch = grp // 2, grp % 2
                    link(nc.vector.tensor_tensor(coef[:, :, :], coef[:, :, :], gates[:, :, 4 * g:4 * g + 4, 1 + branch], ALU.mult))
                    nc.vector.tensor_tensor(o_part[:, :, :, :].rearrange("p h n d -> p (h n) d"), src, flat, ALU.mult).then_inc(o_used, 1)
                    dve.wait_ge(o_used, grp + 1)
                    dst = o_rows[:, :, 256 * g:256 * g + 256]
                    ins = nc.vector.tensor_tensor(dst, dst, o_part[:, :, :, :].rearrange("p h n d -> p h (n d)"), ALU.add)
                    if branch == 1:
                        ins.then_inc(o_ready, 1)
                        dve.wait_ge(o_ready, g + 1)
                    else:
                        link(ins)
                else:
                    g = grp - NSA_JOBS // 2
                    dst = o_rows[:, :, 256 * g:256 * g + 256].rearrange("p h (n d) -> p h n d", d=HD)
                    nc.vector.tensor_tensor(dst, src.rearrange("p (h n) d -> p h n d", h=HALF),
                                            coef[:, :, :].unsqueeze(3).to_broadcast([P, HALF, 4, HD]),
                                            ALU.mult).then_inc(o_used, 1)
                    dve.wait_ge(o_used, grp + 1)

            def attend(jobs, job, j0, t0, a0):
                def outputs_lo(g):
                    dve.wait_ge(a_hi_ready, a0 + g + 1)
                    minus(a_lo[:, :, 2 * g:2 * g + 2, :], oT_ps(g),
                          a_hi[:, :, 2 * g:2 * g + 2, :].bitcast(f32)).then_inc(a_lo_ready, 1)

                for i in range(jobs + 1):
                    if i < jobs:
                        row_maxima(job, j0, i)
                    if i >= 1:
                        dve.wait_ge(pT_done, j0 + i)
                        if j0 + i >= 3:
                            dve.wait_ge(pv_done, j0 + i - 2)
                        nc.vector.tensor_copy(probsT[:, (i - 1) % 2, 512:768], ps[:, 5, 0:256]).then_inc(pT_ready_v, 1)
                    if i >= 3 and i % 2 == 1:
                        gather_group((j0 + i - 3) // 2, j0 == 0)
                outputs_lo(0)
                outputs_lo(1)
                gather_group((j0 + jobs - 2) // 2, j0 == 0)
                outputs_lo(2)
                outputs_lo(3)

            def norm(l, whole, a0):
                def add_residual(half, part):
                    at = slice(512 * part, 512 * (part + 1))
                    return step(nc.vector.scalar_tensor_tensor(x[:, half, at], x[:, half, at], ALPHA,
                                                               ps[:, 4 + 2 * half + part, :], ALU.mult, ALU.add))

                def statistics(half, added):
                    for part in range(2):
                        dve.wait_ge(v_step, added[part])
                        last = step(nc.vector.bn_stats(bn[:, part, :], x[:, half, 512 * part:512 * (part + 1)]))
                    dve.wait_ge(v_step, last)
                    nc.vector.bn_aggr(mean_var[:, l, half, :], bn[:, :, :].rearrange("p a b -> p (a b)")).then_inc(var_ready, 1)
                    dve.wait_ge(var_ready, 2 * l + half + 1)

                def finish(half):
                    for part in range(2):
                        at = slice(512 * part, 512 * (part + 1))
                        last = step(nc.vector.scalar_tensor_tensor(x[:, half, at], x[:, half, at], mean_var[:, l, half, 0:1],
                                                                   gain[:, 0, at], ALU.subtract, ALU.mult))
                    dve.wait_ge(rstd_ready, 2 * l + half + 1)
                    dve.wait_ge(v_step, last)
                    for part in range(2):
                        at = slice(512 * part, 512 * (part + 1))
                        nc.vector.scalar_tensor_tensor(x[:, half, at], x[:, half, at], rstd[:, l, half:half + 1],
                                                       gain[:, 1, at], ALU.mult, ALU.add).then_inc(x_ready, 1)

                def columns_lo(half, part):
                    dve.wait_ge(a_hi_ready, a0 + 2 * half + part + 1)
                    minus(a_lo[:, half, 4 * part:4 * part + 4, :],
                          ps[:, 2 * half + part, :].rearrange("p (k r) -> p k r", k=4),
                          a_hi[:, half, 4 * part:4 * part + 4, :].bitcast(f32)).then_inc(a_lo_ready, 1)

                dve.wait_ge(half_sums, l + 1)
                dve.wait_ge(gain_in, 32 * (l + 1))
                if l == 0:
                    dve.wait_ge(x_in, 16)
                added = [add_residual(0, 0), add_residual(0, 1)]
                statistics(0, added)
                finish(0)
                dve.wait_ge(w_used, whole)
                added = [add_residual(1, 0), add_residual(1, 1)]
                if l < 3:
                    columns_lo(0, 0)
                    columns_lo(0, 1)
                statistics(1, added)
                finish(1)
                if l < 3:
                    columns_lo(1, 0)
                    columns_lo(1, 1)

            def ffn(u0, c0):
                def hidden(c):
                    dve.wait_ge(silu_ready, c0 + c + 1)
                    nc.vector.tensor_tensor(h_rows[:, :, :], silu[:, :, :], ps[:, 0:2, FC:2 * FC],
                                            ALU.mult).then_inc(h_ready, 1)

                def hidden_lo(c):
                    dve.wait_ge(h_hi_ready, c0 + c + 1)
                    minus(h_lo[:, :, :, :], hT_ps, h_hi[:, :, :, :].bitcast(f32)).then_inc(h_lo_ready, 1)

                def rest_in(c, j):
                    rest_of_unit((u0 + j) % SLOTS, 3 * c + (u0 + j + 1))

                hidden(0)
                rest_to(u0 + 4)
                hidden_lo(0)
                rest_to(u0 + 5)
                with dve.Fori(1, NFC - 1) as c:
                    rest_in(c, 2)
                    hidden(c)
                    rest_in(c, 3)
                    hidden_lo(c)
                    rest_in(c, 4)
                units[0] = u0 + 3 * (NFC - 1) + 2
                c = NFC - 1
                rest_to(u0 + 3 * c + 3)
                hidden(c)
                rest_to(min(UNITS, u0 + 3 * c + 4))
                hidden_lo(c)
                rest_to(min(UNITS, u0 + 3 * c + 5))

            attend(**NSA)
            rest_to(U_FF0 + 2)
            norm(0, U_FF0, A_O0)
            rest_to(U_FF0 + 3)
            ffn(U_FF0, 0)
            norm(1, U_MOBA, A_N0)
            rest_to(U_MOBA + 3)
            for n in range(MOBA_CHUNKS):
                if 2 <= n:
                    copy_set(MQ0 + n - 2)
                rest_to(min(U_MOBA + 2 * n + 4, U_WO1 + 3))
                if n < 4:
                    rotate(n % 2, NSA_CHUNKS + n + 1, NSA_CHUNKS - 1 + n + 1, 8)
                rest_to(min(U_MOBA + 2 * n + 5, U_WO1 + 3))
            rest_to(U_WO1 + 3)
            attend(**MOBA)
            rest_to(U_FF1 + 2)
            norm(2, U_FF1, A_O1)
            rest_to(U_FF1 + 3)
            ffn(U_FF1, NFC)
            norm(3, UNITS, None)

        @block.tensor
        def _(pe):
            def product(dst, hi, lo, m_hi, m_lo, start, stop):
                nc.tensor.matmul(dst, hi, m_hi, start=start, stop=False)
                nc.tensor.matmul(dst, hi, m_lo, start=False, stop=False)
                return nc.tensor.matmul(dst, lo, m_hi, start=False, stop=stop)

            def rows_by_weights(u, unit, half, bank):
                s = u % SLOTS
                for k in range(4):
                    at = slice(512 * k, 512 * (k + 1))
                    kt = 4 * unit + k
                    last = product(ps[:, bank, :], a_hi[:, half, kt, :], a_lo[:, half, kt, :],
                                   w_hi[:, s, at], w_lo[:, s, at], start=kt == 0, stop=kt == KT - 1)
                return last

            def chunk(u, banks, count=None, last_use=True):
                for unit in range(2):
                    pe.wait_ge(lo_ready, (u if count is None else count) + unit + 1)
                    for half in range(HALF):
                        last = rows_by_weights(u + unit, unit, half, banks[half])
                    last.then_inc(w_used, 1)

            def first_chunk(u, ready, l):
                for half in range(HALF):
                    if l is not None:
                        for part in range(2):
                            pe.wait_ge(x_ready, 4 * l + 2 * half + part + 1)
                            for k in range(4 * part, 4 * part + 4):
                                last = nc.tensor.transpose(acc_flat[:, 1024 * half + P * k:1024 * half + P * (k + 1)],
                                                           x[:, half, P * k:P * (k + 1)], ident[:, :])
                            last.then_inc(xT_done, 1)
                    for unit in range(2):
                        if l is None:
                            pe.wait_ge(a_lo_ready, half + 1)
                        else:
                            pe.wait_ge(a_lo_ready, ready + 2 * half + unit + 1)
                        pe.wait_ge(lo_ready, u + unit + 1)
                        last = rows_by_weights(u + unit, unit, half, half)
                        if half == 1:
                            last.then_inc(w_used, 1)

            def set_free(k):
                if k > Q0:
                    pe.wait_ge(set_a, k - 2)
                pe.wait_ge(set_v, k)

            def turn_rows(k, b):
                for t in range(4):
                    for half in range(HALF):
                        last = nc.tensor.transpose(set_ps[:, t, P * half:P * (half + 1)],
                                                   rows[:, b, half, P * t:P * (t + 1)], ident[:, :])
                last.then_inc(turned, 1)

            def turn_twice(g0, dst):
                for g in range(KV):
                    for half in range(HALF):
                        last = nc.tensor.transpose(dst[:, g, P * half:P * (half + 1)],
                                                   twice[:, half, g0 + g, :, :].rearrange("p t d -> p (t d)"), ident[:, :])
                last.then_inc(turned, 1)

            first_chunk(0, 0, None)
            chunk(2, (2, 3))
            pe.wait_ge(consts, 1)
            pe.wait_ge(twice_ready, 1)
            turn_twice(0, set_ps)
            turn_twice(4, ps[:, 6:8, :].rearrange("p b (t r) -> p (b t) r", r=S))
            pe.wait_ge(evac, 1)
            chunk(4, (0, 1))
            pe.wait_ge(roped, 2)
            set_free(Q0)
            turn_rows(Q0, 1)
            pe.wait_ge(w1_in, 32)
            for kv in range(2):
                for m in range(2):
                    at = (2 * kv + m) * 64
                    for j in range(CS):
                        last = nc.tensor.matmul(ps[:, 6, at:at + KV * NCMP], w1_sb[:, kv, j, P * m:P * (m + 1)],
                                                blocks[:, kv, j, :, :].rearrange("p g n -> p (g n)"),
                                                start=j == 0, stop=j == CS - 1)
            last.then_inc(hid_done, 1)
            pe.wait_ge(evac, 2)
            chunk(6, (2, 3))
            pe.wait_ge(roped, 3)
            set_free(Q1)
            turn_rows(Q1, 0)
            pe.wait_ge(rep_ready, 1)
            for m in range(2):
                nc.tensor.matmul(ps[:, 7, 0:64], w2k_sb[:, m, :, :].rearrange("p t d -> p (t d)"),
                                 hidT[:, 0, m, :, :].rearrange("p g n -> p (g n)"), start=m == 0, stop=m == 1)
            for hb in range(2):
                for m in range(2):
                    last = nc.tensor.matmul(ps[:, 7, 64 * (hb + 1):64 * (hb + 2)], hid_rep[:, m, hb, :], w2v_sb[:, m, :],
                                            start=m == 0, stop=m == 1)
            last.then_inc(kv_cmp_done, 1)
            pe.wait_ge(wg_lo_ready, 1)
            pe.wait_ge(hid_ready, 1)
            for half in range(HALF):
                for k in range(KT):
                    last = product(ps[:, 6, 48 * half:48 * (half + 1)], a_hi[:, half, k, :], a_lo[:, half, k, :],
                                   wg_hi[:, k, :], wg_lo[:, k, :], start=k == 0, stop=k == KT - 1)
            last.then_inc(gates_done, 1)
            pe.wait_ge(set_a, 2)
            pe.wait_ge(set_v, Q1 + 1)
            pe.wait_ge(kv_cmp_ready, 1)
            for half in range(HALF):
                for t in range(8):
                    at = 256 * half + 32 * t
                    last = nc.tensor.matmul(ps[:, 7, at:at + 32], qT[:, t, P * half:P * (half + 1)],
                                            kcz[:, t // 2, :, :].rearrange("p t n -> p (t n)"), start=True, stop=True)
            last.then_inc(s_cmp_done, 1)
            pe.wait_ge(evac, 3)
            chunk(8, (0, 1))
            pe.wait_ge(gates_ready, 1)
            pe.wait_ge(e_cmp_ready, 1)
            for hb in range(2):
                for half in range(HALF):
                    at = P * (2 * hb + half)
                    last = nc.tensor.transpose(ps[:, 6, at:at + P],
                                               e_cmp[:, half, 8 * hb:8 * hb + 8, :].rearrange("p n c -> p (n c)"), ident[:, :])
            last.then_inc(e_cmpT_done, 1)
            pe.wait_ge(twice_ready, 2)
            turn_twice(0, set_ps)
            pe.wait_ge(evac, 4)
            turn_twice(4, win_ps)
            pe.wait_ge(e_cmpT_ready, 1)
            pe.wait_ge(set_a, KS - 1)
            pe.wait_ge(set_v, KS + 1)
            for half in range(HALF):
                for hb in range(2):
                    last = nc.tensor.matmul(ps[:, 4 + 2 * half + hb, :], e_cmpT[:, hb, half, :],
                                            vcz[:, hb, :, :].rearrange("p n d -> p (n d)"), start=True, stop=True)
            last.then_inc(o_cmp_done, 1)
            pe.wait_ge(evac, 5)
            set_free(MQ0)

            def scores(job, j0, i):
                q, k, _, _, _ = job(i)
                b = i % 2
                if j0 + i >= 2:
                    pe.wait_ge(p_ready, j0 + i - 1)
                for half in range(HALF):
                    keys = P * (half + 1)
                    dst = ps[:, 2 - 2 * half + b, 0:2 * keys]
                    nc.tensor.matmul(dst, qT[:, q, P * half:P * (half + 1)], kz[:, k, :, 0:keys],
                                     start=True, stop=False)
                    last = nc.tensor.matmul(dst.rearrange("p (h k) -> p h k", h=2)[:, :, keys - P:keys],
                                            ident_b[:, :], causal[:, :, :], start=False, stop=True)
                last.then_inc(s_ready, 1)

            def turn_probs(i_all):
                b = i_all % 2
                pe.wait_ge(p_ready, i_all + 1)
                if i_all == 0:
                    pe.wait_ge(o_cmp_used, 1)
                else:
                    pe.wait_ge(pT_ready_a, i_all)
                    pe.wait_ge(pT_ready_v, i_all)
                for h in range(2):
                    for half in range(HALF):
                        at = 256 * half + h * P * (half + 1)
                        nc.tensor.transpose(acc_flat[:, 2048 + P * (2 * h + half):2048 + P * (2 * h + half + 1)],
                                            probs[:, b, at:at + P], ident[:, :])
                for h in range(2):
                    at = 256 + h * S + P
                    last = nc.tensor.transpose(acc_flat[:, 2560 + P * h:2560 + P * (h + 1)], probs[:, b, at:at + P], ident[:, :])
                last.then_inc(pT_done, 1)

            def weigh_values(job, j0, i):
                _, _, cols, grp, j = job(i)
                b = i % 2
                if j0 > 0 and i == 0:
                    pe.wait_ge(evac, NSA_CHUNKS + MOBA_CHUNKS)
                pe.wait_ge(pT_ready_a, j0 + i + 1)
                pe.wait_ge(pT_ready_v, j0 + i + 1)
                if grp >= 2:
                    pe.wait_ge(o_used, grp - 1)
                bank = 6 + grp % 2
                for h in range(2):
                    for half in range(HALF):
                        at = 256 * half + HD * (2 * j + h)
                        dst = ps[:, bank, at:at + HD]
                        c = slice(cols[h], cols[h] + HD)
                        last = nc.tensor.matmul(dst, probsT[:, b, P * (2 * h + half):P * (2 * h + half + 1)],
                                                values[:, 0, c], start=True, stop=half == 0)
                        if half == 1:
                            last = nc.tensor.matmul(dst, probsT[:, b, 512 + P * h:512 + P * (h + 1)], values[:, 1, c],
                                                    start=False, stop=True)
                last.then_inc(pv_done, 1)

            def turn_outputs(g, t0):
                if t0 == 0:
                    pe.wait_ge(o_ready, g + 1)
                else:
                    pe.wait_ge(o_used, NSA_JOBS // 2 + g + 1)
                for half in range(HALF):
                    for t in range(2):
                        last = nc.tensor.transpose(oT_ps(g)[:, half, t, :],
                                                   o_rows[:, half, 256 * g + P * t:256 * g + P * (t + 1)], ident[:, :])
                last.then_inc(oT_done, 1)

            def attend(jobs, job, j0, t0, a0):
                scores(job, j0, 0)
                scores(job, j0, 1)
                for i in range(jobs):
                    turn_probs(j0 + i)
                    if i + 2 < jobs:
                        scores(job, j0, i + 2)
                    if i == jobs - 1:
                        for g in range(3):
                            turn_outputs(g, t0)
                    weigh_values(job, j0, i)
                turn_outputs(3, t0)

            def output_weights(u, a0):
                for unit in range(2):
                    pe.wait_ge(a_lo_ready, a0 + 2 * unit + 2)
                    pe.wait_ge(lo_ready, u + unit + 1)
                    for half in range(HALF):
                        last = rows_by_weights(u + unit, unit, half, 4 + 2 * half)
                    last.then_inc(w_used, 1)
                for half in range(HALF):
                    for unit in range(2):
                        pe.wait_ge(lo_ready, u + 2 + unit + 1)
                        last = rows_by_weights(u + 2 + unit, unit, half, 5 + 2 * half)
                        if half == 1:
                            last.then_inc(w_used, 1)
                    if half == 0:
                        last.then_inc(half_sums, 1)

            def ffn(u0, c0, ready, l):
                def down(s, start, stop):
                    for half in range(HALF):
                        for k in range(2):
                            for part in range(3):
                                for c in range(2):
                                    at = slice(1024 * k + 512 * c, 1024 * k + 512 * (c + 1))
                                    last = nc.tensor.matmul(
                                        ps[:, 4 + 2 * half + c, :], (h_hi, h_hi, h_lo)[part][:, half, k, :],
                                        (w_hi, w_lo, w_hi)[part][:, s, at],
                                        start=start and k == 0 and part == 0, stop=stop and k == 1 and part == 2)
                        if stop and half == 0:
                            last.then_inc(half_sums, 1)
                    last.then_inc(w_used, 1)

                def turn_hidden(c):
                    pe.wait_ge(h_ready, c0 + c + 1)
                    for half in range(HALF):
                        for t in range(2):
                            last = nc.tensor.transpose(hT_ps[:, half, t, :], h_rows[:, half, P * t:P * (t + 1)], ident[:, :])
                    last.then_inc(hT_done, 1)

                def step(c, start=False):
                    chunk(u0 + 2, (0, 1), count=3 * c + (u0 - 1))
                    pe.wait_ge(h_lo_ready, c0 + c)
                    pe.wait_ge(lo_ready, 3 * c + (u0 + 2))
                    down((u0 + 1) % SLOTS, start, False)
                    turn_hidden(c)

                first_chunk(u0, ready, l)
                turn_hidden(0)
                step(1, start=True)
                with pe.Fori(2, NFC) as c:
                    step(c)
                pe.wait_ge(h_lo_ready, c0 + NFC)
                pe.wait_ge(lo_ready, u0 + 3 * NFC)
                down((u0 + 3 * NFC - 1) % SLOTS, False, True)

            attend(**NSA)
            output_weights(U_WO0, A_X)
            ffn(U_FF0, 0, A_O0, 0)
            for n in range(MOBA_CHUNKS):
                if n == 0:
                    first_chunk(U_MOBA, A_N0, 1)
                else:
                    if n >= 2:
                        pe.wait_ge(evac, NSA_CHUNKS + n - 1)
                    b = MOBA_BANKS[n]
                    chunk(U_MOBA + 2 * n, (b, b + 1))
                if 1 <= n < 5:
                    pe.wait_ge(roped, NSA_CHUNKS - 1 + n)
                    set_free(MQ0 + n - 1)
                    turn_rows(MQ0 + n - 1, (n - 1) % 2)
            pe.wait_ge(evac, NSA_CHUNKS + MOBA_CHUNKS - 1)
            set_free(MK1 + 1)
            attend(**MOBA)
            output_weights(U_WO1, A_N1)
            ffn(U_FF1, NFC, A_O1, 2)


def _unit(block):
    return block.reshape(-1, P, block.shape[-1]).transpose(1, 0, 2).reshape(P, -1)


def _columns(w, lo, hi):
    return [_unit(w[512 * i:512 * (i + 1), lo:hi]) for i in range(2)]


def _network(wg, wu, wd):
    units = []
    for c in range(NFC):
        at = slice(FC * c, FC * (c + 1))
        units += _columns(np.concatenate([wg[:, at], wu[:, at]], axis=1), 0, 2 * FC)
        if c > 0:
            units.append(_unit(wd[FC * (c - 1):FC * c]))
    units.append(_unit(wd[FC * (NFC - 1):]))
    return units


def kernel(x, positions, nsa_w_in, nsa_w_o, nsa_ck_pos, nsa_ck_w1, nsa_ck_w2, nsa_cv_pos, nsa_cv_w1, nsa_cv_w2,
           moba_w_in, moba_w_o, ffn_wg, ffn_wu, ffn_wd, ln1_g, ln1_b, ln2_g, ln2_b):
    import concourse.bacc as bacc
    from concourse.bass_utils import run_bass_kernel_spmd

    a = {k: np.asarray(v) for k, v in locals().items() if k not in ("bacc", "run_bass_kernel_spmd")}
    w_in, w_moba = a["nsa_w_in"][0], a["moba_w_in"][0]
    kv = NH * HD
    part = [w_in[:, kv + 256 * i:kv + 256 * (i + 1)] for i in range(6)]
    chunks = [np.concatenate([part[0], part[1]], axis=1), w_in[:, 0:512], w_in[:, 512:1024],
              np.concatenate([part[2], part[4]], axis=1), np.concatenate([part[3], part[5]], axis=1)]
    units = [u for c in chunks for u in _columns(c, 0, 512)]
    for c in range(2):
        units += _columns(a["nsa_w_o"][0], 512 * c, 512 * (c + 1))
    units += _network(a["ffn_wg"][0], a["ffn_wu"][0], a["ffn_wd"][0])
    for c in range(MOBA_CHUNKS):
        units += _columns(w_moba, 512 * c, 512 * (c + 1))
    for c in range(2):
        units += _columns(a["moba_w_o"][0], 512 * c, 512 * (c + 1))
    units += _network(a["ffn_wg"][1], a["ffn_wu"][1], a["ffn_wd"][1])

    def halves(w):
        return w.reshape(2, CS, HD, -1).transpose(0, 2, 1, 3).reshape(P, CS, -1)

    rows = a["x"][0].reshape(HALF, P, D)
    arrays = {
        "x_rows": rows.transpose(1, 0, 2),
        "x_cols": rows.reshape(HALF, P, KT, P).transpose(3, 0, 2, 1).reshape(P, HALF, KT * P),
        "stream": np.stack(units),
        "w_gates": w_in[:, kv + 6 * KV * HD:].reshape(KT, P, 3 * NH).transpose(1, 0, 2),
        "w1": np.stack([halves(a["nsa_ck_w1"][0]), halves(a["nsa_cv_w1"][0])], axis=1),
        "w2": np.stack([a[n][0].reshape(2, P, HD).transpose(1, 0, 2) for n in ("nsa_ck_w2", "nsa_cv_w2")], axis=1),
        "cpos": np.stack([a[n][0].reshape(2, CS, HD).transpose(0, 2, 1).reshape(P, CS)
                          for n in ("nsa_ck_pos", "nsa_cv_pos")], axis=1),
        "positions": a["positions"][0].reshape(HALF, P).transpose(1, 0),
        "norms": np.stack([np.stack([a[f"ln{i}_{p}"][l] for p in "gb"]) for l in range(2) for i in (1, 2)]),
    }
    nc = bacc.Bacc("TRN2", target_bir_lowering=False, num_devices=1)
    ins = {}
    for name, value in arrays.items():
        arrays[name] = np.ascontiguousarray(value)
        ins[name] = nc.dram_tensor(name, arrays[name].shape, mybir.dt.from_np(arrays[name].dtype),
                                   kind="ExternalInput").ap()
    out = nc.dram_tensor("out", [HALF, P, D], mybir.dt.float32, kind="ExternalOutput").ap()
    build(nc, ins["x_rows"], ins["x_cols"], ins["stream"], ins["w_gates"],
          ins["w1"], ins["w2"], ins["cpos"], ins["positions"], ins["norms"], out)
    result = run_bass_kernel_spmd(nc, [arrays], core_ids=[0])
    return result.results[0]["out"].reshape(1, S, D)
```

```python
import math
from contextlib import ExitStack

import numpy as np
import concourse.bass as bass
from concourse import mybir

S = 256
D = 1024
HD = 64
NH = 16
KV = 4
HALF = 2
P = 128
KT = D // P
FF = 2816
FC = 256
NFC = FF // FC
CB = 32
CS = 16
NCMP = (S - CB) // CS + 1
HID = 256
ROPE = HD // 4
THETA = 500000.0
ALPHA = (2 * 2) ** 0.25
EPS = 1e-5
SCALE = HD ** -0.5
NEG = -1e30
UNIT = 2048
SLOTS = 3
NSA_CHUNKS = 5
MOBA_CHUNKS = 6
U_NSA = 0
U_WO0 = U_NSA + 2 * NSA_CHUNKS
U_FF0 = U_WO0 + 4
U_MOBA = U_FF0 + 3 * NFC
U_WO1 = U_MOBA + 2 * MOBA_CHUNKS
U_FF1 = U_WO1 + 4
UNITS = U_FF1 + 3 * NFC
NSA_JOBS = 16
MOBA_JOBS = 8
JOBS = NSA_JOBS + MOBA_JOBS


def build(nc, x_rows, x_cols, stream, w_gates, w1, w2, cpos, positions, norms, out):
    f32 = mybir.dt.float32
    f32r = mybir.dt.float32r
    bf16 = mybir.dt.bfloat16
    i32 = mybir.dt.int32
    ALU = mybir.AluOpType
    ACT = mybir.ActivationFunctionType
    AX = mybir.AxisListType

    with ExitStack() as ctx:
        def sb(name, shape, dt=f32):
            return ctx.enter_context(nc.sbuf_tensor(name, shape, dt))

        def sem(name):
            return ctx.enter_context(nc.semaphore(name))

        raw = sb("raw", [P, SLOTS, UNIT])
        w_hi = sb("w_hi", [P, SLOTS, UNIT], f32r)
        w_lo = sb("w_lo", [P, SLOTS, UNIT], f32r)
        x = sb("x", [P, HALF, D])
        a_hi = sb("a_hi", [P, HALF, KT, P], f32r)
        a_lo = sb("a_lo", [P, HALF, KT, P], f32r)
        kz = sb("kz", [P, 8, 2, S])
        qT = sb("qT", [P, 8, S])
        rows = sb("rows", [P, 2, HALF, 512])
        twice = sb("twice", [P, HALF, 8, 2, HD])
        arena = sb("arena", [P, 2 * CS * HID])
        values = arena[:, 0:3072].rearrange("p (h n) -> p h n", h=HALF)
        probs = arena[:, 3072:4608].rearrange("p (b n) -> p b n", b=2)
        probsT = arena[:, 4608:6144].rearrange("p (b n) -> p b n", b=2)
        silu = arena[:, 6144:6656].rearrange("p (h n) -> p h n", h=HALF)
        h_rows = arena[:, 6656:7168].rearrange("p (h n) -> p h n", h=HALF)
        hid_rep = arena[:, 6656:7168].rearrange("p (m b n) -> p m b n", m=2, b=2)
        hid_rows = arena[:, 7168:7680]
        e_cmp = arena[:, 7168:7680].rearrange("p (h n c) -> p h n c", h=HALF, c=16)
        e_cmpT = arena[:, 7680:8192].rearrange("p (b h r) -> p b h r", b=2, h=HALF)
        w1_sb = arena[:, :].rearrange("p (a j n) -> p a j n", a=2, n=HID)
        gain = sb("gain", [P, 2, D])
        h_hi = sb("h_hi", [P, HALF, 2, P], f32r)
        h_lo = sb("h_lo", [P, HALF, 2, P], f32r)
        last_hi = sb("last_hi", [P, HALF, 2, P], f32r)
        last_lo = sb("last_lo", [P, HALF, 2, P], f32r)
        blocks_mem = sb("blocks_mem", [P, 2 * CS * KV * NCMP])
        blocks = blocks_mem[:, :].rearrange("p (t j g n) -> p t j g n", t=2, j=CS, g=KV)
        hidT = sb("hidT", [P, 2, 2, KV, 16])
        w2k_sb = sb("w2k_sb", [P, 2, 2, HD])
        w2v_sb = sb("w2v_sb", [P, 2, HD])
        wg_raw = sb("wg_raw", [P, KT, 48])
        wg_hi = sb("wg_hi", [P, KT, 48], f32r)
        wg_lo = sb("wg_lo", [P, KT, 48], f32r)
        cpos_sb = sb("cpos_sb", [P, 2, CS])
        kcz = sb("kcz", [P, KV, 2, 16])
        vcz = blocks_mem[:, 0:1024].rearrange("p (b n d) -> p b n d", b=2, d=HD)
        cmp_stat = sb("cmp_stat", [P, 4, HALF * NH])
        gates = sb("gates", [P, HALF, NH, 3])
        neg_max = sb("neg_max", [P, JOBS, HALF, 2])
        sums = sb("sums", [P, JOBS, HALF, 2])
        coef = sb("coef", [P, JOBS, HALF, 2])
        pos_i = sb("pos_i", [P, HALF], i32)
        pos_f = sb("pos_f", [P, HALF])
        inv = sb("inv", [P, 16])
        phase = sb("phase", [P, 2, 16])
        ang = sb("ang", [P, 3, HALF, 16])
        cos2 = sb("cos2", [P, HALF, 16])
        sin2 = sb("sin2", [P, HALF, 16])
        turn = sb("turn", [P, 2, HALF, 8, 16])
        ident = sb("ident", [P, P])
        ident_b = sb("ident_b", [P, P], bf16)
        causal = sb("causal", [P, 2, P], bf16)
        cmp_mask = sb("cmp_mask", [P, HALF, 16])
        row_ok = sb("row_ok", [P, HALF])
        own_head = sb("own_head", [P, 8])
        bn = sb("bn", [P, 2, 6])
        mean_var = sb("mean_var", [P, 4, HALF, 2])
        var_eps = sb("var_eps", [P, 4, HALF])
        rstd = sb("rstd", [P, 4, HALF])
        minus_half = sb("minus_half", [P, 1])
        ps = ctx.enter_context(nc.psum_tensor("ps", [P, 8, 512], f32))

        raw_in = [sem(f"raw_in{s}") for s in range(SLOTS)]
        hi_ready = sem("hi_ready")
        lo_ready = sem("lo_ready")
        w_used = sem("w_used")
        xT_in = [sem(f"xT_in{q}") for q in range(4)]
        first_in = [sem(f"first_in{u}") for u in range(2)]
        first_hi = sem("first_hi")
        first_lo = sem("first_lo")
        warm = sem("warm")
        x_in = sem("x_in")
        small_in = sem("small_in")
        w1_in = sem("w1_in")
        gain_in = sem("gain_in")
        consts = sem("consts")
        a_hi_ready = sem("a_hi_ready")
        a_lo_ready = sem("a_lo_ready")
        wg_hi_ready = sem("wg_hi_ready")
        wg_lo_ready = sem("wg_lo_ready")
        evac = sem("evac")
        roped = sem("roped")
        twice_ready = sem("twice_ready")
        turned = sem("turned")
        set_a = sem("set_a")
        set_v = sem("set_v")
        angles_ready = sem("angles_ready")
        sincos_ready = sem("sincos_ready")
        hid_done = sem("hid_done")
        hid_rows_ready = sem("hid_rows_ready")
        hidT_done = sem("hidT_done")
        hid_ready = sem("hid_ready")
        rep_ready = sem("rep_ready")
        kv_cmp_done = sem("kv_cmp_done")
        kv_cmp_ready = sem("kv_cmp_ready")
        gates_done = sem("gates_done")
        gates_ready = sem("gates_ready")
        s_cmp_done = sem("s_cmp_done")
        s_cmp_ready = sem("s_cmp_ready")
        e_cmp_ready = sem("e_cmp_ready")
        e_cmp_scaled = sem("e_cmp_scaled")
        e_cmpT_done = sem("e_cmpT_done")
        e_cmpT_ready = sem("e_cmpT_ready")
        v_zero = sem("v_zero")
        s_ready = sem("s_ready")
        max_ready = sem("max_ready")
        p_ready = sem("p_ready")
        p_scaled = sem("p_scaled")
        pT_done = sem("pT_done")
        pT_ready_a = sem("pT_ready_a")
        pT_ready_v = sem("pT_ready_v")
        pv_done = sem("pv_done")
        silu_ready = sem("silu_ready")
        first_sums = sem("first_sums")
        first_silu = sem("first_silu")
        first_h = sem("first_h")
        h_ready = sem("h_ready")
        hT_done = sem("hT_done")
        h_hi_ready = sem("h_hi_ready")
        h_lo_ready = sem("h_lo_ready")
        sums_done = sem("sums_done")
        var_ready = sem("var_ready")
        rstd_ready = sem("rstd_ready")
        x_ready = sem("x_ready")
        xT_done = sem("xT_done")
        v_step = sem("v_step")
        g_step = sem("g_step")
        stored = sem("stored")

        block = ctx.enter_context(nc.Block())

        SMALL = 6
        A_X, A_O0, A_N0, A_N1, A_O1 = 4, 12, 16, 20, 28
        KC, VC, Q0, Q1, KS, KW, MQ0, MQ1, MK0, MK1 = range(10)

        X_QUARTERS = ((0, 0), (1, 0), (0, 1), (1, 1))

        def nsa_job(i):
            t, branch = i // 2, i % 2
            s = branch * KV + t // 2
            return t, s, (128 * s + 64, 128 * s), branch == 0, branch == 1

        def moba_job(i):
            return i, i, (192 * i, 192 * i + 64), True, True

        NSA = dict(jobs=NSA_JOBS, job=nsa_job, j0=0, a0=A_X, u=U_WO0)
        MOBA = dict(jobs=MOBA_JOBS, job=moba_job, j0=NSA_JOBS, a0=A_N1, u=U_WO1)

        MOBA_BANKS = [0, 2, 0, 2, 6, 6]
        SUM_BANK = [0, 4, 0, 4]

        acc_flat = ps[:, :, :].rearrange("p b n -> p (b n)")
        x_cols_raw = twice[:, :, :, :, :].rearrange("p h g t d -> p h (g t d)")

        def x_quarter(of, q):
            half, part = X_QUARTERS[q]
            return of[:, half, 512 * part:512 * (part + 1)]

        a_hi_flat = a_hi[:, :, :, :].rearrange("p h k r -> p h (k r)")
        a_lo_flat = a_lo[:, :, :, :].rearrange("p h k r -> p h (k r)")
        set_ps = ps[:, 4:6, :].rearrange("p b (t r) -> p (b t) r", r=S)
        hT_ps = ps[:, 2, :].rearrange("p (h t r) -> p h t r", h=HALF, t=2)

        def out_ps(t):
            return ps[:, 6 + t % 2, 0:S].rearrange("p (h r) -> p h r", h=HALF)

        win_ps = ps[:, 2:4, :].rearrange("p b (t r) -> p (b t) r", r=S)

        def set_target(k, lo, hi):
            if k in (Q0, Q1, MQ0, MQ1):
                i = k % 2 if k >= MQ0 else k - Q0
                return qT[lo:hi, 4 * i:4 * i + 4, :]
            i = (k - KS) if k < MQ0 else k - MK0
            return kz[lo:hi, 4 * i:4 * i + 4, lo // HD, :]

        @block.sync
        def _(sp):
            def load_x(q):
                sp.dma_start(x_quarter(x_cols_raw, q), x_quarter(x_cols, q)).then_inc(xT_in[q], 16)

            def load_half(u, part):
                at = slice(UNIT // 2 * part, UNIT // 2 * (part + 1))
                sp.dma_start(raw[:, u, at], stream[u, :, at]).then_inc(first_in[u] if part == 0 else raw_in[u], 16)

            load_x(0)
            load_half(0, 0)
            load_x(1)
            load_half(0, 1)
            load_x(2)
            load_half(1, 0)
            load_x(3)
            load_half(1, 1)
            sp.dma_start(pos_i[:, :], positions).then_inc(small_in, 16)
            sp.dma_start(wg_raw[:, :, :], w_gates).then_inc(small_in, 16)
            sp.dma_start(cpos_sb[:, :, :], cpos).then_inc(small_in, 16)
            sp.dma_start(w2k_sb[:, :, 0, :], w2[:, 0, :, :]).then_inc(small_in, 16)
            sp.dma_start(w2k_sb[:, :, 1, :], w2[:, 0, :, :]).then_inc(small_in, 16)
            sp.dma_start(w2v_sb[:, :, :], w2[:, 1, :, :]).then_inc(small_in, 16)
            sp.dma_start(raw[:, 2, :], stream[2]).then_inc(raw_in[2], 16)
            with sp.Fori(1, UNITS // SLOTS) as t:
                for s in range(SLOTS):
                    sp.wait_ge(lo_ready, (t - 1) * SLOTS + s + 1)
                    unit = stream[bass.ds(t * SLOTS + s, 1), :, :].rearrange("a p n -> (a p) n")
                    sp.dma_start(raw[:, s, :], unit).then_inc(raw_in[s], 16)
            for part in range(4):
                sp.wait_ge(x_ready, 12 + part + 1)
                half, at = part // 2, slice(512 * (part % 2), 512 * (part % 2 + 1))
                sp.dma_start(out[half, :, at], x[:, half, at]).then_inc(stored, 16)
            sp.wait_ge(stored, 16 * 4)

        @block.gpsimd
        def _(gp):
            steps = [0]

            def link(ins):
                steps[0] += 1
                ins.then_inc(g_step, 1)
                gp.wait_ge(g_step, steps[0])

            nc.gpsimd.memset(minus_half[:, :], -0.5).then_inc(warm, 1)
            freqs = np.power(np.float32(THETA), -np.arange(0, ROPE, 2, dtype=np.float32) / np.float32(ROPE))
            for j in range(ROPE // 2):
                nc.gpsimd.memset(inv[:, j:j + 1], float(freqs[j]))
                nc.gpsimd.memset(inv[:, 8 + j:9 + j], float(freqs[j]))
            nc.gpsimd.memset(phase[:, :, 0:8], 0.0)
            nc.gpsimd.memset(phase[:, 0, 8:16], 0.25)
            nc.gpsimd.memset(phase[:, 1, 8:16], math.pi / 2)
            nc.gpsimd.memset(row_ok[:, :], 1.0)
            nc.gpsimd.memset(own_head[:, :], 1.0)
            nc.gpsimd.memset(causal[:, :, :], 0.0)
            nc.gpsimd.memset(cmp_mask[:, :, :], 0.0)
            nc.gpsimd.memset(hidT[:, :, :, :, :], 0.0)
            nc.gpsimd.memset(kcz[:, :, :, :], 0.0)
            nc.gpsimd.memset(ident_b[:, :], 0.0)
            link(nc.gpsimd.memset(ident[:, :], 0.0))
            for m in (ident, ident_b):
                nc.gpsimd.affine_select(out=m[:, :], in_=m[:, :], compare_op=ALU.not_equal, fill=1.0, base=0,
                                        pattern=[[-1, P]], channel_multiplier=1)
            nc.gpsimd.affine_select(out=causal[:, :, :], in_=causal[:, :, :], compare_op=ALU.is_ge, fill=NEG,
                                    base=0, pattern=[[0, 2], [-1, P]], channel_multiplier=1)
            nc.gpsimd.affine_select(out=cmp_mask[:, :, :], in_=cmp_mask[:, :, :], compare_op=ALU.is_ge, fill=NEG,
                                    base=1 - CB, pattern=[[P, HALF], [-CS, 16]], channel_multiplier=1)
            nc.gpsimd.affine_select(out=row_ok[:, :], in_=row_ok[:, :], compare_op=ALU.is_ge, fill=0.0,
                                    base=1 - CB, pattern=[[P, HALF]], channel_multiplier=1)
            link(nc.gpsimd.affine_select(out=own_head[:, :], in_=own_head[:, :], compare_op=ALU.is_ge, fill=0.0,
                                         base=0, pattern=[[-16, 8]], channel_multiplier=1))
            nc.gpsimd.affine_select(out=own_head[:, :], in_=own_head[:, :], compare_op=ALU.is_ge, fill=0.0,
                                    base=15, pattern=[[16, 8]], channel_multiplier=-1).then_inc(consts, 1)
            nc.gpsimd.memset(kz[:, :, :, :], 0.0).then_inc(consts, 1)

            def load_gain(l):
                gp.dma_start(gain[:, 0, :], norms[l, 0:1, :].to_broadcast([P, D])).then_inc(gain_in, 16)
                gp.dma_start(gain[:, 1, :], norms[l, 1:2, :].to_broadcast([P, D])).then_inc(gain_in, 16)

            def roots(l):
                for half in range(HALF):
                    gp.wait_ge(var_ready, 2 * l + half + 1)
                    link(nc.gpsimd.tensor_scalar(var_eps[:, l, half:half + 1], mean_var[:, l, half, 1:2],
                                                 1.0, EPS, ALU.mult, ALU.add))
                    nc.gpsimd.tensor_tensor(rstd[:, l, half:half + 1], var_eps[:, l, half:half + 1],
                                            minus_half[:, :], ALU.pow).then_inc(rstd_ready, 1)
                if l < 3:
                    gp.wait_ge(x_ready, 4 * (l + 1))
                    load_gain(l + 1)

            load_gain(0)
            gp.wait_ge(hid_done, 1)
            nc.gpsimd.memset(values, 0.0).then_inc(v_zero, 1)
            roots(0)
            gp.wait_ge(pv_done, NSA_JOBS)
            nc.gpsimd.memset(values, 0.0).then_inc(v_zero, 1)
            roots(1)
            roots(2)
            roots(3)

        @block.scalar
        def _(act):
            units = [0]

            def copy(dst, src, scale=1.0):
                return nc.scalar.activation(dst, src, ACT.Copy, scale=scale)

            def round_unit(s, arrived, used):
                act.wait_ge(raw_in[s], arrived)
                if used is not None:
                    act.wait_ge(w_used, used)
                copy(w_hi[:, s, :], raw[:, s, :]).then_inc(hi_ready, 1)

            def round_to(end):
                for u in range(units[0], end):
                    round_unit(u % SLOTS, 16 * (u // SLOTS + 1), u - SLOTS + 1 if u >= SLOTS else None)
                units[0] = max(units[0], end)

            def write_twice(b, lo, hi):
                for t in range(2):
                    last = copy(twice[:, :, lo:hi, t, :],
                                rows[:, b, :, HD * lo:HD * hi].rearrange("p h (g d) -> p h g d", d=HD))
                return last

            def copy_set(k):
                act.wait_ge(turned, k + 1)
                if k == Q0:
                    act.wait_ge(consts, 2)
                copy(set_target(k, 0, HD), (win_ps if k == KW else set_ps)[0:HD]).then_inc(set_a, 1)

            act.wait_ge(warm, 1)
            copy(cmp_stat[:, 3, 0:1], minus_half[:, :])

            def x_hi(q):
                act.wait_ge(xT_in[q], 16)
                copy(x_quarter(a_hi_flat, q), x_quarter(x_cols_raw, q)).then_inc(a_hi_ready, 1)

            def half_hi(u, part):
                at = slice(UNIT // 2 * part, UNIT // 2 * (part + 1))
                if part == 0:
                    act.wait_ge(first_in[u], 16)
                else:
                    act.wait_ge(raw_in[u], 16)
                copy(w_hi[:, u, at], raw[:, u, at]).then_inc(first_hi if part == 0 else hi_ready, 1)

            x_hi(0)
            half_hi(0, 0)
            x_hi(1)
            half_hi(0, 1)
            x_hi(2)
            half_hi(1, 0)
            x_hi(3)
            half_hi(1, 1)
            units[0] = 2
            round_to(3)
            act.wait_ge(angles_ready, 1)
            nc.scalar.activation(ang[:, 2], ang[:, 1], ACT.Sin).then_inc(sincos_ready, 1)

            def load_w1(piece):
                at = slice(CS // 2 * (piece % 2), CS // 2 * (piece % 2 + 1))
                act.dma_start(w1_sb[:, piece // 2, at], w1[:, piece // 2, at]).then_inc(w1_in, 16)

            load_w1(0)
            act.wait_ge(small_in, 16 * SMALL)
            copy(wg_hi[:, :, :], wg_raw[:, :, :]).then_inc(wg_hi_ready, 1)
            round_to(4)
            load_w1(1)

            act.wait_ge(w_used, 2)
            copy(rows[:, 0, :, :], ps[:, 0:2, :]).then_inc(evac, 1)
            round_to(5)
            load_w1(2)
            act.wait_ge(evac, 1)
            act.wait_ge(a_lo_ready, A_X)
            write_twice(0, 4, 8)
            act.wait_ge(roped, 1)
            write_twice(0, 0, 4).then_inc(twice_ready, 1)
            act.wait_ge(gates_done, 1)
            nc.scalar.activation(gates[:, :, :, :].rearrange("p h n c -> p h (n c)"),
                                 ps[:, 6, 0:96].rearrange("p (h n) -> p h n", h=HALF),
                                 ACT.Sigmoid).then_inc(gates_ready, 1)
            round_to(6)
            load_w1(3)
            act.wait_ge(w_used, 4)
            copy(rows[:, 1, :, :], ps[:, 2:4, :], SCALE).then_inc(evac, 1)
            round_to(8)
            act.wait_ge(w_used, 6)
            copy(rows[:, 0, :, :], ps[:, 0:2, :], SCALE).then_inc(evac, 1)
            copy_set(Q0)
            round_to(9)
            act.wait_ge(hid_done, 1)
            nc.scalar.activation(hid_rows[0:KV * NCMP, :], ps[0:KV * NCMP, 6, :],
                                 ACT.Gelu_apprx_tanh).then_inc(hid_rows_ready, 1)
            act.wait_ge(hidT_done, 1)
            copy(hidT[:, :, :, :, 0:NCMP].rearrange("p k m g n -> p (k m) g n"),
                 ps[:, 6, 0:256].rearrange("p (a c) -> p a c", c=64)[:, :, 0:KV * NCMP]
                 .rearrange("p a (g n) -> p a g n", n=NCMP)).then_inc(hid_ready, 1)
            round_to(10)
            act.wait_ge(w_used, 8)
            copy(rows[:, 1, :, :], ps[:, 2:4, :]).then_inc(evac, 1)
            copy_set(Q1)
            act.wait_ge(roped, 4)
            write_twice(1, 0, 8).then_inc(twice_ready, 1)
            round_to(11)
            act.wait_ge(s_cmp_ready, 1)
            nc.scalar.activation(e_cmp[:, :, :, :], e_cmp[:, :, :, :], ACT.Exp).then_inc(e_cmp_ready, 1)
            copy_set(KS)
            copy_set(KW)
            round_to(U_WO0 + 2)
            act.wait_ge(e_cmpT_done, 1)
            copy(e_cmpT, ps[:, 1, :].rearrange("p (b h r) -> p b h r", b=2, h=HALF)).then_inc(e_cmpT_ready, 1)
            act.dma_start(x[:, :, :], x_rows).then_inc(x_in, 16)

            def attend(jobs, job, j0, a0, u, evacuate_values):
                def exp(i):
                    b = i % 2
                    act.wait_ge(max_ready, j0 + i + 1)
                    if i >= 2:
                        act.wait_ge(pT_done, j0 + i - 1)
                    for half in range(HALF):
                        keys = P * (half + 1)
                        for h in range(2):
                            at = 2 * P * half + h * keys
                            last = nc.scalar.activation(probs[:, b, at:at + keys],
                                                        ps[:, 2 - 2 * half + b, h * keys:(h + 1) * keys], ACT.Exp,
                                                        bias=neg_max[:, j0 + i, half, h:h + 1],
                                                        accum_out=sums[:, j0 + i, half, h:h + 1])
                    last.then_inc(p_ready, 1)

                def outputs_hi(i):
                    act.wait_ge(pv_done, j0 + i + 1)
                    t = job(i)[0]
                    copy(a_hi[:, :, t, :], out_ps(t)).then_inc(a_hi_ready, 1)

                exp(0)
                exp(1)
                round_to(u + 2)
                evacuate_values()
                for i in range(jobs):
                    if i >= 2 and job(i - 2)[4]:
                        outputs_hi(i - 2)
                    if i == jobs - 2:
                        round_to(u + 3)
                    act.wait_ge(pT_done, j0 + i + 1)
                    if i >= 2:
                        act.wait_ge(pv_done, j0 + i - 1)
                    copy(probsT[:, i % 2, 0:512], ps[:, 4, :]).then_inc(pT_ready_a, 1)
                    if i + 2 < jobs:
                        exp(i + 2)
                round_to(u + 4)
                for i in range(jobs - 2, jobs):
                    if job(i)[4]:
                        outputs_hi(i)

            def norm_hi(l, u):
                round_to(u + 2)
                for half in range(HALF):
                    for part in range(2):
                        act.wait_ge(xT_done, 4 * l + 2 * half + part + 1)
                        copy(a_hi[:, half, 4 * part:4 * part + 4, :],
                             ps[:, 4 - SUM_BANK[l] + 2 * half + part, :].rearrange("p (k r) -> p k r", k=4)
                             ).then_inc(a_hi_ready, 1)
                    if half == 0:
                        round_to(u + 3)

            def ffn(u0, c0):
                def silu_of(c, whole):
                    act.wait_ge(w_used, whole)
                    nc.scalar.activation(silu[:, :, :], ps[:, 0:2, 0:FC], ACT.Silu).then_inc(silu_ready, 1)

                def hidden_hi(c, hi=h_hi):
                    act.wait_ge(hT_done, c0 + c + 1)
                    copy(hi[:, :, :, :], hT_ps).then_inc(h_hi_ready, 1)

                def round_in(c, j):
                    round_unit((u0 + j) % SLOTS, ((u0 + j) // SLOTS + 1) * 16 + c * 16, 3 * c + (u0 + j - 2))

                act.wait_ge(first_sums, u0 // U_FF1 + 1)
                nc.scalar.activation(silu[:, 0, :], ps[:, 0, 0:FC], ACT.Silu).then_inc(first_silu, 1)
                act.wait_ge(w_used, u0 + 2)
                nc.scalar.activation(silu[:, 1, :], ps[:, 1, 0:FC], ACT.Silu).then_inc(silu_ready, 1)
                round_to(u0 + 4)
                hidden_hi(0)
                round_to(u0 + 5)
                with act.Fori(1, NFC - 1) as c:
                    round_in(c, 2)
                    silu_of(c, 3 * c + (u0 + 1))
                    round_in(c, 3)
                    hidden_hi(c)
                    round_in(c, 4)
                units[0] = u0 + 3 * (NFC - 1) + 2
                c = NFC - 1
                round_to(u0 + 3 * c + 3)
                silu_of(c, u0 + 3 * c + 1)
                hidden_hi(c, last_hi)
                round_to(min(UNITS, u0 + 3 * c + 5))

            def nsa_values():
                act.wait_ge(w_used, U_WO0)
                act.wait_ge(v_zero, 1)
                copy(values[:, :, 0:1024].rearrange("p h (n t d) -> p h n t d", t=2, d=HD)[:, :, :, 1, :],
                     ps[:, 6:8, :].rearrange("p h (n d) -> p h n d", d=HD)).then_inc(evac, 1)

            def moba_values(n):
                act.wait_ge(w_used, U_MOBA + 2 * (4 + n) + 2)
                tiles = values[:, :, 768 * n:768 * (n + 1)].rearrange("p h (t c) -> p h t c", c=192)
                sums_of = ps[:, 6:8, :].rearrange("p h (t j d) -> p h t j d", j=2, d=HD)
                for j in range(2):
                    last = copy(tiles[:, :, :, 128 * j:128 * j + HD], sums_of[:, :, :, j, :])
                last.then_inc(evac, 1)

            attend(**NSA, evacuate_values=nsa_values)
            norm_hi(0, U_FF0)
            ffn(U_FF0, 0)
            norm_hi(1, U_MOBA)
            for n in range(MOBA_CHUNKS - 1):
                if 2 <= n:
                    copy_set(MQ0 + n - 2)
                round_to(min(U_MOBA + 2 * n + 4, U_WO1))
                act.wait_ge(w_used, U_MOBA + 2 * n + 2)
                b = n % 2
                if n in (2, 3):
                    act.wait_ge(turned, MQ0 + n - 1)
                if n < 4:
                    copy(rows[:, b, :, :], ps[:, 2 * b:2 * b + 2, :], SCALE if n < 2 else 1.0).then_inc(evac, 1)
                else:
                    act.wait_ge(v_zero, 2)
                    moba_values(0)
                round_to(min(U_MOBA + 2 * n + 5, U_WO1))
            copy_set(MK1)
            round_to(U_WO1)
            attend(**MOBA, evacuate_values=lambda: moba_values(1))
            norm_hi(2, U_FF1)
            ffn(U_FF1, NFC)

        @block.vector
        def _(dve):
            steps = [0]
            units = [0]

            def link(ins):
                steps[0] += 1
                ins.then_inc(v_step, 1)
                dve.wait_ge(v_step, steps[0])

            def step(ins):
                steps[0] += 1
                ins.then_inc(v_step, 1)
                return steps[0]

            def minus(dst, a, b):
                return nc.vector.tensor_tensor(dst, a, b, ALU.subtract)

            def rest_of_unit(s, rounded):
                dve.wait_ge(hi_ready, rounded)
                minus(w_lo[:, s, :], raw[:, s, :], w_hi[:, s, :].bitcast(f32)).then_inc(lo_ready, 1)

            def rest_to(end):
                for u in range(units[0], end):
                    rest_of_unit(u % SLOTS, u + 1)
                units[0] = max(units[0], end)

            def rotate(b, chunks, count, heads):
                dve.wait_ge(evac, chunks)
                r = rows[:, b, :, 0:heads * HD].rearrange("p h (n d) -> p h n d", d=HD)
                t, u = turn[:, 0, :, 0:heads, :], turn[:, 1, :, 0:heads, :]

                def wide(table, lo, hi):
                    return table[:, :, lo:hi].unsqueeze(2).to_broadcast([P, HALF, heads, hi - lo])
                nc.vector.tensor_tensor(t, r[:, :, :, 0:16], wide(cos2, 0, 16), ALU.mult)
                nc.vector.tensor_tensor(u[:, :, :, 0:8], r[:, :, :, 8:16], wide(sin2, 0, 8), ALU.mult)
                link(nc.vector.tensor_tensor(u[:, :, :, 8:16], r[:, :, :, 0:8], wide(sin2, 8, 16), ALU.mult))
                nc.vector.tensor_tensor(r[:, :, :, 0:16], t, u, ALU.add).then_inc(roped, 1)
                dve.wait_ge(roped, count)

            def copy_set(k):
                dve.wait_ge(turned, k + 1)
                nc.vector.tensor_copy(set_target(k, HD, P), (win_ps if k == KW else set_ps)[HD:P]).then_inc(set_v, 1)

            def x_lo(q):
                dve.wait_ge(a_hi_ready, q + 1)
                minus(x_quarter(a_lo_flat, q), x_quarter(x_cols_raw, q),
                      x_quarter(a_hi_flat, q).bitcast(f32)).then_inc(a_lo_ready, 1)

            def half_lo(u, part):
                at = slice(UNIT // 2 * part, UNIT // 2 * (part + 1))
                dve.wait_ge(first_hi if part == 0 else hi_ready, u + 1)
                minus(w_lo[:, u, at], raw[:, u, at],
                      w_hi[:, u, at].bitcast(f32)).then_inc(first_lo if part == 0 else lo_ready, 1)

            x_lo(0)
            half_lo(0, 0)
            x_lo(1)
            half_lo(0, 1)
            x_lo(2)
            half_lo(1, 0)
            x_lo(3)
            half_lo(1, 1)
            units[0] = 2
            dve.wait_ge(small_in, 16 * SMALL)
            dve.wait_ge(consts, 1)
            link(nc.vector.tensor_copy(pos_f[:, :], pos_i[:, :]))
            link(nc.vector.tensor_tensor(ang[:, 0], pos_f[:, :].unsqueeze(2).to_broadcast([P, HALF, 16]),
                                         inv[:, :].unsqueeze(1).to_broadcast([P, HALF, 16]), ALU.mult))
            link(nc.vector.scalar_tensor_tensor(ang[:, 1], ang[:, 0], 1.0 / (2 * math.pi),
                                                phase[:, 0:1, :].to_broadcast([P, HALF, 16]), ALU.mult, ALU.add))
            ROUND = 1.5 * 2.0 ** 23
            link(nc.vector.tensor_scalar(ang[:, 1], ang[:, 1], ROUND, None, ALU.add))
            link(nc.vector.tensor_scalar(ang[:, 1], ang[:, 1], ROUND, None, ALU.subtract))
            C1 = 6.28125
            C2 = float(np.floor((2 * math.pi - C1) * 2 ** 20) / 2 ** 20)
            C3 = 2 * math.pi - C1 - C2
            for part in (C1, C2, C3):
                link(nc.vector.scalar_tensor_tensor(ang[:, 0], ang[:, 1], -part, ang[:, 0], ALU.mult, ALU.add))
            link(nc.vector.tensor_tensor(ang[:, 0], ang[:, 0], phase[:, 1:2, :].to_broadcast([P, HALF, 16]), ALU.add))
            LIMIT = 3.1415925
            nc.vector.tensor_scalar(ang[:, 1], ang[:, 0], LIMIT, -LIMIT, ALU.min, ALU.max).then_inc(angles_ready, 1)
            rest_to(3)
            dve.wait_ge(wg_hi_ready, 1)
            minus(wg_lo[:, :, :], wg_raw[:, :, :], wg_hi[:, :, :].bitcast(f32)).then_inc(wg_lo_ready, 1)
            dve.wait_ge(sincos_ready, 1)
            nc.vector.tensor_copy(cos2[:, :, 0:8], ang[:, 2, :, 8:16])
            nc.vector.tensor_copy(cos2[:, :, 8:16], ang[:, 2, :, 8:16])
            nc.vector.tensor_scalar(sin2[:, :, 0:8], ang[:, 2, :, 0:8], -1.0, None, ALU.mult)
            link(nc.vector.tensor_copy(sin2[:, :, 8:16], ang[:, 2, :, 0:8]))
            rest_to(4)

            rotate(0, 1, 1, KV)
            rest_to(6)
            rotate(1, 2, 2, 8)
            for kv, k in ((0, KC), (1, VC)):
                dve.wait_ge(turned, k + 1)
                for part in range(2):
                    lo = HD * part
                    src = ps[lo:lo + HD, 4 + 2 * kv:6 + 2 * kv, :].rearrange("p b (g n j) -> p j (b g) n", n=16, j=CS)
                    last = nc.vector.tensor_tensor(
                        blocks[lo:lo + HD, kv, :, :, :], src[:, :, :, part:part + NCMP],
                        cpos_sb[lo:lo + HD, kv, :].unsqueeze(2).unsqueeze(3).to_broadcast([HD, CS, KV, NCMP]), ALU.add)
                last.then_inc(set_v, 1)
            rest_to(8)
            rotate(0, 3, 3, 8)
            copy_set(Q0)
            rest_to(9)
            dve.wait_ge(hid_ready, 1)
            for m in range(2):
                last = nc.vector.tensor_copy(
                    hid_rep[:, m, :, :].rearrange("p b (g r n) -> p (b g) r n", g=2, r=4),
                    hidT[:, 1, m, :, :].unsqueeze(2).to_broadcast([P, KV, 4, 16]))
            last.then_inc(rep_ready, 1)
            rest_to(10)
            rotate(1, 4, 4, 8)
            copy_set(Q1)
            dve.wait_ge(kv_cmp_done, 1)
            for part in range(2):
                lo = HD * part
                nc.vector.tensor_copy(kcz[lo:lo + HD, :, part, :],
                                      ps[lo:lo + HD, 1, 0:64].rearrange("p (g n) -> p g n", g=KV))
            for hb in range(2):
                last = nc.vector.tensor_tensor(
                    vcz[:, hb, :, :], ps[:, 1, 64 * (hb + 1):64 * (hb + 2)].unsqueeze(1).to_broadcast([P, 8, HD]),
                    own_head[:, :].unsqueeze(2).to_broadcast([P, 8, HD]), ALU.mult)
            last.then_inc(kv_cmp_ready, 1)
            dve.wait_ge(s_cmp_done, 1)
            link(nc.vector.tensor_tensor(
                e_cmp[:, :, :, :], ps[:, 1, :].rearrange("p (h n c) -> p h n c", h=HALF, c=16),
                cmp_mask[:, :, :].unsqueeze(2).to_broadcast([P, HALF, NH, 16]), ALU.add))
            link(nc.vector.tensor_reduce(cmp_stat[:, 0, :].rearrange("p (h n) -> p h n", h=HALF), e_cmp, AX.X, ALU.max))
            minus(e_cmp, e_cmp, cmp_stat[:, 0, :].rearrange("p (h n) -> p h n", h=HALF).unsqueeze(3)
                  .to_broadcast([P, HALF, NH, 16])).then_inc(s_cmp_ready, 1)
            dve.wait_ge(e_cmp_ready, 1)
            link(nc.vector.tensor_reduce(cmp_stat[:, 1, :].rearrange("p (h n) -> p h n", h=HALF), e_cmp, AX.X, ALU.add))
            link(nc.vector.reciprocal(cmp_stat[:, 2, :], cmp_stat[:, 1, :]))
            dve.wait_ge(gates_ready, 1)
            by_head = cmp_stat[:, 2:4, :].rearrange("p s (h n) -> p s h n", h=HALF)
            link(nc.vector.tensor_tensor(by_head[:, 1], by_head[:, 0], gates[:, :, :, 0], ALU.mult))
            link(nc.vector.tensor_tensor(by_head[:, 0], by_head[:, 1],
                                         row_ok[:, :].unsqueeze(2).to_broadcast([P, HALF, NH]), ALU.mult))
            nc.vector.tensor_tensor(e_cmp[:, :, :, :], e_cmp[:, :, :, :], by_head[:, 0].unsqueeze(3).to_broadcast([P, HALF, NH, 16]),
                                    ALU.mult).then_inc(e_cmp_scaled, 1)
            copy_set(KS)
            copy_set(KW)
            rest_to(U_WO0 + 2)

            def attend(jobs, job, j0, a0, u):
                def row_maxima(i):
                    b = i % 2
                    dve.wait_ge(s_ready, j0 + i + 1)
                    for half in range(HALF):
                        keys = P * (half + 1)
                        last = nc.vector.tensor_reduce(
                            neg_max[:, j0 + i, half, :],
                            ps[:, 2 - 2 * half + b, 0:2 * keys].rearrange("p (h k) -> p h k", h=2), AX.X, ALU.max, negate=True)
                    last.then_inc(max_ready, 1)

                def scale_probs(i):
                    dve.wait_ge(p_ready, j0 + i + 1)
                    link(nc.vector.reciprocal(coef[:, j0 + i, :, :], sums[:, j0 + i, :, :]))
                    if j0 == 0:
                        t, branch = i // 2, i % 2
                        link(nc.vector.tensor_tensor(coef[:, i, :, :], coef[:, i, :, :],
                                                     gates[:, :, 2 * t:2 * t + 2, 1 + branch], ALU.mult))
                    for half in range(HALF):
                        keys = P * (half + 1)
                        for h in range(2):
                            at = slice(2 * P * half + h * keys, 2 * P * half + (h + 1) * keys)
                            last = nc.vector.tensor_scalar(probs[:, i % 2, at], probs[:, i % 2, at],
                                                           coef[:, j0 + i, half, h:h + 1], None, ALU.mult)
                    last.then_inc(p_scaled, 1)

                def outputs_lo(i):
                    t = job(i)[0]
                    dve.wait_ge(a_hi_ready, a0 + t + 1)
                    minus(a_lo[:, :, t, :], out_ps(t), a_hi[:, :, t, :].bitcast(f32)).then_inc(a_lo_ready, 1)

                row_maxima(0)
                row_maxima(1)
                scale_probs(0)
                rest_to(u + 2)
                for i in range(jobs):
                    if i >= 2 and job(i - 2)[4]:
                        outputs_lo(i - 2)
                    if i + 2 < jobs:
                        row_maxima(i + 2)
                    dve.wait_ge(pT_done, j0 + i + 1)
                    if i >= 2:
                        dve.wait_ge(pv_done, j0 + i - 1)
                    nc.vector.tensor_copy(probsT[:, i % 2, 512:768], ps[:, 5, 0:256]).then_inc(pT_ready_v, 1)
                    if i + 1 < jobs:
                        scale_probs(i + 1)
                    if i == jobs - 2:
                        rest_to(u + 3)
                rest_to(u + 4)
                for i in range(jobs - 2, jobs):
                    if job(i)[4]:
                        outputs_lo(i)

            def norm(l, u, a0):
                def quarter_sums(half, part):
                    if half == 1 and (part == 1 or l % 2 == 0):
                        dve.wait_ge(w_used, u - 1 + part)
                    else:
                        dve.wait_ge(sums_done, 5 * (l // 2) + 2 * (l % 2) + 2 * half + part + 1)

                def add_residual(half, part):
                    at = slice(512 * part, 512 * (part + 1))
                    quarter_sums(half, part)
                    return step(nc.vector.scalar_tensor_tensor(x[:, half, at], x[:, half, at], ALPHA,
                                                               ps[:, SUM_BANK[l] + 2 * half + part, :], ALU.mult, ALU.add))

                def quarter_statistics(half, part):
                    dve.wait_ge(v_step, add_residual(half, part))
                    return step(nc.vector.bn_stats(bn[:, part, :], x[:, half, 512 * part:512 * (part + 1)]))

                def last_quarter_statistics(half):
                    dve.wait_ge(v_step, quarter_statistics(half, 1))
                    nc.vector.bn_aggr(mean_var[:, l, half, :], bn[:, :, :].rearrange("p a b -> p (a b)")).then_inc(var_ready, 1)
                    dve.wait_ge(var_ready, 2 * l + half + 1)

                def finish(half):
                    for part in range(2):
                        at = slice(512 * part, 512 * (part + 1))
                        last = step(nc.vector.scalar_tensor_tensor(x[:, half, at], x[:, half, at], mean_var[:, l, half, 0:1],
                                                                   gain[:, 0, at], ALU.subtract, ALU.mult))
                    dve.wait_ge(rstd_ready, 2 * l + half + 1)
                    dve.wait_ge(v_step, last)
                    for part in range(2):
                        at = slice(512 * part, 512 * (part + 1))
                        nc.vector.scalar_tensor_tensor(x[:, half, at], x[:, half, at], rstd[:, l, half:half + 1],
                                                       gain[:, 1, at], ALU.mult, ALU.add).then_inc(x_ready, 1)

                def columns_lo(half, part):
                    dve.wait_ge(a_hi_ready, a0 + 2 * half + part + 1)
                    minus(a_lo[:, half, 4 * part:4 * part + 4, :],
                          ps[:, 4 - SUM_BANK[l] + 2 * half + part, :].rearrange("p (k r) -> p k r", k=4),
                          a_hi[:, half, 4 * part:4 * part + 4, :].bitcast(f32)).then_inc(a_lo_ready, 1)

                dve.wait_ge(gain_in, 32 * (l + 1))
                if l == 0:
                    dve.wait_ge(x_in, 16)
                quarter_statistics(0, 0)
                last_quarter_statistics(0)
                finish(0)
                if l < 3:
                    rest_to(u + 1)
                quarter_statistics(1, 0)
                if l < 3:
                    columns_lo(0, 0)
                    columns_lo(0, 1)
                    rest_to(u + 2)
                last_quarter_statistics(1)
                finish(1)
                if l < 3:
                    columns_lo(1, 0)
                    columns_lo(1, 1)

            def ffn(u0, c0):
                def hidden(c):
                    dve.wait_ge(silu_ready, c0 + c + 1)
                    nc.vector.tensor_tensor(h_rows[:, :, :], silu[:, :, :], ps[:, 0:2, FC:2 * FC],
                                            ALU.mult).then_inc(h_ready, 1)

                def hidden_lo(c, hi=h_hi, lo=h_lo):
                    dve.wait_ge(h_hi_ready, c0 + c + 1)
                    minus(lo[:, :, :, :], hT_ps, hi[:, :, :, :].bitcast(f32)).then_inc(h_lo_ready, 1)

                def rest_in(c, j):
                    rest_of_unit((u0 + j) % SLOTS, 3 * c + (u0 + j + 1))

                dve.wait_ge(first_silu, u0 // U_FF1 + 1)
                nc.vector.tensor_tensor(h_rows[:, 0, :], silu[:, 0, :], ps[:, 0, FC:2 * FC], ALU.mult).then_inc(first_h, 1)
                dve.wait_ge(silu_ready, c0 + 1)
                nc.vector.tensor_tensor(h_rows[:, 1, :], silu[:, 1, :], ps[:, 1, FC:2 * FC], ALU.mult).then_inc(h_ready, 1)
                rest_to(u0 + 4)
                hidden_lo(0)
                rest_to(u0 + 5)
                with dve.Fori(1, NFC - 1) as c:
                    rest_in(c, 2)
                    hidden(c)
                    rest_in(c, 3)
                    hidden_lo(c)
                    rest_in(c, 4)
                units[0] = u0 + 3 * (NFC - 1) + 2
                c = NFC - 1
                rest_to(u0 + 3 * c + 3)
                hidden(c)
                hidden_lo(c, last_hi, last_lo)
                rest_to(min(UNITS, u0 + 3 * c + 4))

            attend(**NSA)
            norm(0, U_FF0, A_O0)
            rest_to(U_FF0 + 3)
            ffn(U_FF0, 0)
            rest_to(U_MOBA + 1)
            norm(1, U_MOBA, A_N0)
            rest_to(U_MOBA + 3)
            for n in range(MOBA_CHUNKS - 1):
                if 2 <= n:
                    copy_set(MQ0 + n - 2)
                rest_to(min(U_MOBA + 2 * n + 4, U_WO1))
                if n < 4:
                    rotate(n % 2, NSA_CHUNKS + n + 1, NSA_CHUNKS - 1 + n + 1, 8)
                rest_to(min(U_MOBA + 2 * n + 5, U_WO1))
            copy_set(MK1)
            rest_to(U_WO1)
            attend(**MOBA)
            norm(2, U_FF1, A_O1)
            rest_to(U_FF1 + 3)
            ffn(U_FF1, NFC)
            norm(3, UNITS, None)

        @block.tensor
        def _(pe):
            def product(dst, hi, lo, m_hi, m_lo, start, stop):
                nc.tensor.matmul(dst, hi, m_hi, start=start, stop=False)
                nc.tensor.matmul(dst, hi, m_lo, start=False, stop=False)
                return nc.tensor.matmul(dst, lo, m_hi, start=False, stop=stop)

            def rows_by_weights(u, unit, half, bank, tiles=range(4)):
                s = u % SLOTS
                for k in tiles:
                    at = slice(512 * k, 512 * (k + 1))
                    kt = 4 * unit + k
                    last = product(ps[:, bank, :], a_hi[:, half, kt, :], a_lo[:, half, kt, :],
                                   w_hi[:, s, at], w_lo[:, s, at], start=kt == 0, stop=kt == KT - 1)
                return last

            def one_unit(u, unit, banks, halves=(0, 1), count=None):
                pe.wait_ge(lo_ready, (u if count is None else count) + unit + 1)
                for half in halves:
                    last = rows_by_weights(u + unit, unit, half, banks[half])
                if 1 in halves:
                    last.then_inc(w_used, 1)

            def chunk(u, banks, count=None):
                for unit in range(2):
                    one_unit(u, unit, banks, count=count)

            def turn_x(l, half):
                for part in range(2):
                    pe.wait_ge(x_ready, 4 * l + 2 * half + part + 1)
                    for k in range(4 * part, 4 * part + 4):
                        at = 512 * (4 - SUM_BANK[l]) + 1024 * half + P * k
                        last = nc.tensor.transpose(acc_flat[:, at:at + P], x[:, half, P * k:P * (k + 1)], ident[:, :])
                    last.then_inc(xT_done, 1)

            def first_chunk(u, ready, l):
                for half in range(HALF):
                    if half == 1:
                        turn_x(l, half)
                    for unit in range(2):
                        pe.wait_ge(a_lo_ready, ready + 2 * half + unit + 1)
                        pe.wait_ge(lo_ready, u + unit + 1)
                        last = rows_by_weights(u + unit, unit, half, half)
                        if half == 1:
                            last.then_inc(w_used, 1)
                    if half == 0 and l % 2 == 0:
                        last.then_inc(first_sums, 1)

            def set_free(k):
                if k > Q0:
                    pe.wait_ge(set_a, k - 2)
                pe.wait_ge(set_v, k)

            def turn_rows(k, b):
                for t in range(4):
                    for half in range(HALF):
                        last = nc.tensor.transpose(set_ps[:, t, P * half:P * (half + 1)],
                                                   rows[:, b, half, P * t:P * (t + 1)], ident[:, :])
                last.then_inc(turned, 1)

            def turn_twice(g0, dst):
                for g in range(KV):
                    for half in range(HALF):
                        last = nc.tensor.transpose(dst[:, g, P * half:P * (half + 1)],
                                                   twice[:, half, g0 + g, :, :].rearrange("p t d -> p (t d)"), ident[:, :])
                last.then_inc(turned, 1)

            for u in range(2):
                for part, split in ((0, first_lo), (1, lo_ready)):
                    pe.wait_ge(split, u + 1)
                    for half in range(HALF):
                        pe.wait_ge(a_lo_ready, 2 * u + half + 1)
                        last = rows_by_weights(u, u, half, half, tiles=range(2 * part, 2 * part + 2))
                last.then_inc(w_used, 1)
            one_unit(2, 0, (2, 3))
            pe.wait_ge(wg_lo_ready, 1)
            for half in range(HALF):
                one_unit(2, 1, (2, 3), halves=(half,))
                for k in range(KT):
                    last = product(ps[:, 6, 48 * half:48 * (half + 1)], a_hi[:, half, k, :], a_lo[:, half, k, :],
                                   wg_hi[:, k, :], wg_lo[:, k, :], start=k == 0, stop=k == KT - 1)
            last.then_inc(gates_done, 1)
            pe.wait_ge(consts, 1)
            pe.wait_ge(twice_ready, 1)
            turn_twice(0, set_ps)
            pe.wait_ge(gates_ready, 1)
            turn_twice(4, ps[:, 6:8, :].rearrange("p b (t r) -> p (b t) r", r=S))
            pe.wait_ge(evac, 1)
            chunk(4, (0, 1))
            pe.wait_ge(roped, 2)
            set_free(Q0)
            turn_rows(Q0, 1)
            pe.wait_ge(w1_in, 16 * 4)
            for kv in range(2):
                for j in range(CS):
                    last = nc.tensor.matmul(ps[0:KV * NCMP, 6, HID * kv:HID * (kv + 1)],
                                            blocks[:, kv, j, :, :].rearrange("p g n -> p (g n)"), w1_sb[:, kv, j, :],
                                            start=j == 0, stop=j == CS - 1)
            last.then_inc(hid_done, 1)
            pe.wait_ge(evac, 2)
            one_unit(6, 0, (2, 3))
            pe.wait_ge(hid_rows_ready, 1)
            for a in range(4):
                last = nc.tensor.transpose(ps[:, 6, 64 * a:64 * a + KV * NCMP],
                                           hid_rows[0:KV * NCMP, P * a:P * (a + 1)], ident[0:KV * NCMP, 0:KV * NCMP])
            last.then_inc(hidT_done, 1)
            one_unit(6, 1, (2, 3))
            pe.wait_ge(roped, 3)
            set_free(Q1)
            turn_rows(Q1, 0)
            pe.wait_ge(rep_ready, 1)
            pe.wait_ge(evac, 3)
            for m in range(2):
                nc.tensor.matmul(ps[:, 1, 0:64], w2k_sb[:, m, :, :].rearrange("p t d -> p (t d)"),
                                 hidT[:, 0, m, :, :].rearrange("p g n -> p (g n)"), start=m == 0, stop=m == 1)
            for hb in range(2):
                for m in range(2):
                    last = nc.tensor.matmul(ps[:, 1, 64 * (hb + 1):64 * (hb + 2)], hid_rep[:, m, hb, :], w2v_sb[:, m, :],
                                            start=m == 0, stop=m == 1)
            last.then_inc(kv_cmp_done, 1)
            pe.wait_ge(hid_ready, 1)
            one_unit(8, 0, (6, 7), halves=(0,))
            pe.wait_ge(set_a, 2)
            pe.wait_ge(set_v, Q1 + 1)
            pe.wait_ge(kv_cmp_ready, 1)
            for half in range(HALF):
                for t in range(8):
                    at = 256 * half + 32 * t
                    last = nc.tensor.matmul(ps[:, 1, at:at + 32], qT[:, t, P * half:P * (half + 1)],
                                            kcz[:, t // 2, :, :].rearrange("p t n -> p (t n)"), start=True, stop=True)
            last.then_inc(s_cmp_done, 1)
            one_unit(8, 0, (6, 7), halves=(1,))
            pe.wait_ge(twice_ready, 2)
            turn_twice(0, set_ps)
            pe.wait_ge(evac, 4)
            turn_twice(4, win_ps)

            def scores(job, j0, i):
                q, k = job(i)[:2]
                b = i % 2
                if j0 + i >= 2:
                    pe.wait_ge(p_ready, j0 + i - 1)
                for half in range(HALF):
                    keys = P * (half + 1)
                    dst = ps[:, 2 - 2 * half + b, 0:2 * keys]
                    nc.tensor.matmul(dst, qT[:, q, P * half:P * (half + 1)], kz[:, k, :, 0:keys],
                                     start=True, stop=False)
                    last = nc.tensor.matmul(dst.rearrange("p (h k) -> p h k", h=2)[:, :, keys - P:keys],
                                            ident_b[:, :], causal[:, :, :], start=False, stop=True)
                last.then_inc(s_ready, 1)

            def turn_probs(i_all):
                b = i_all % 2
                pe.wait_ge(p_scaled, i_all + 1)
                if i_all > 0:
                    pe.wait_ge(pT_ready_a, i_all)
                    pe.wait_ge(pT_ready_v, i_all)
                for h in range(2):
                    for half in range(HALF):
                        at = 256 * half + h * P * (half + 1)
                        nc.tensor.transpose(acc_flat[:, 2048 + P * (2 * h + half):2048 + P * (2 * h + half + 1)],
                                            probs[:, b, at:at + P], ident[:, :])
                for h in range(2):
                    at = 256 + h * S + P
                    last = nc.tensor.transpose(acc_flat[:, 2560 + P * h:2560 + P * (h + 1)], probs[:, b, at:at + P], ident[:, :])
                last.then_inc(pT_done, 1)

            def weigh_values(job, j0, i, a0):
                t, _, cols, first, last_one = job(i)
                b = i % 2
                pe.wait_ge(pT_ready_a, j0 + i + 1)
                pe.wait_ge(pT_ready_v, j0 + i + 1)
                if t >= 2 and first:
                    pe.wait_ge(a_lo_ready, a0 + t - 1)
                dst = ps[:, 6 + t % 2, 0:S]
                if j0 == 0 and first:
                    nc.tensor.matmul(dst, vcz[:, t // 4, 2 * (t % 4):2 * (t % 4) + 2, :].rearrange("p n d -> p (n d)"),
                                     e_cmpT[:, t // 4, :, :].rearrange("p h r -> p (h r)"), start=True, stop=False)
                for h in range(2):
                    c = slice(cols[h], cols[h] + P)
                    nc.tensor.matmul(dst, values[:, 0, c], probsT[:, b, S * h:S * (h + 1)],
                                     start=j0 > 0 and h == 0, stop=False)
                    last = nc.tensor.matmul(dst[:, P:S], values[:, 1, c], probsT[:, b, 512 + P * h:512 + P * (h + 1)],
                                            start=False, stop=last_one and h == 1)
                last.then_inc(pv_done, 1)

            def attend(jobs, job, j0, a0, u):
                for i in range(jobs):
                    if i + 2 < jobs:
                        scores(job, j0, i + 2)
                    else:
                        if i == jobs - 2:
                            pe.wait_ge(lo_ready, u + 1)
                            pe.wait_ge(a_lo_ready, a0 + 4)
                            pe.wait_ge(p_ready, j0 + jobs - 1)
                        half = i - (jobs - 2)
                        last = rows_by_weights(u, 0, half, 2 * half)
                        if half == 1:
                            last.then_inc(w_used, 1)
                    turn_probs(j0 + i)
                    if i == 1:
                        pe.wait_ge(evac, NSA_CHUNKS + (MOBA_CHUNKS if j0 > 0 else 0))
                        if j0 == 0:
                            pe.wait_ge(e_cmpT_ready, 1)
                    if i >= 1:
                        weigh_values(job, j0, i - 1, a0)
                weigh_values(job, j0, jobs - 1, a0)

            def output_weights(u, a0, l):
                for half in range(HALF):
                    for unit, tiles, c in ((1, 0, 1), (2, 1, 0), (3, 1, 1)):
                        pe.wait_ge(lo_ready, u + unit + 1)
                        if unit == 2:
                            pe.wait_ge(a_lo_ready, a0 + 8)
                        if unit == 3 and half == 1:
                            turn_x(l, 0)
                        last = rows_by_weights(u + unit, tiles, half, 2 * half + c)
                        if half == 1:
                            last.then_inc(w_used, 1)
                        elif unit > 1:
                            last.then_inc(sums_done, 1)

            def ffn(u0, c0, ready, l):
                def down_part(s, half, k, hi, lo, start, stop, c):
                    at = slice(1024 * k + 512 * c, 1024 * k + 512 * (c + 1))
                    return product(ps[:, 4 + 2 * half + c, :], hi[:, half, k, :], lo[:, half, k, :],
                                   w_hi[:, s, at], w_lo[:, s, at], start=start, stop=stop)

                def down(s, start):
                    for half in range(HALF):
                        for k in range(2):
                            for c in range(2):
                                last = down_part(s, half, k, h_hi, h_lo, start and k == 0, False, c)
                    last.then_inc(w_used, 1)

                def turn_hidden(c):
                    pe.wait_ge(h_ready, c0 + c + 1)
                    for half in range(HALF):
                        for t in range(2):
                            last = nc.tensor.transpose(hT_ps[:, half, t, :], h_rows[:, half, P * t:P * (t + 1)], ident[:, :])
                    last.then_inc(hT_done, 1)

                def step(c):
                    chunk(u0 + 2, (0, 1), count=3 * c + (u0 - 1))
                    pe.wait_ge(h_lo_ready, c0 + c)
                    pe.wait_ge(lo_ready, 3 * c + (u0 + 2))
                    down((u0 + 1) % SLOTS, False)
                    turn_hidden(c)

                first_chunk(u0, ready, l)
                pe.wait_ge(lo_ready, u0 + 3)
                pe.wait_ge(first_h, u0 // U_FF1 + 1)
                rows_by_weights(u0 + 2, 0, 0, 0)
                turn_hidden(0)
                rows_by_weights(u0 + 2, 0, 1, 1).then_inc(w_used, 1)
                pe.wait_ge(lo_ready, u0 + 4)
                for half in range(HALF):
                    last = rows_by_weights(u0 + 3, 1, half, half)
                last.then_inc(w_used, 1)
                pe.wait_ge(h_lo_ready, c0 + 1)
                pe.wait_ge(lo_ready, u0 + 5)
                down((u0 + 4) % SLOTS, True)
                turn_hidden(1)
                with pe.Fori(2, NFC - 1) as c:
                    step(c)
                c = NFC - 1
                s_before, s_last = (u0 + 3 * c + 1) % SLOTS, (u0 + 3 * c + 2) % SLOTS
                chunk(u0 + 3 * c - 1, (0, 1))
                pe.wait_ge(h_lo_ready, c0 + c)
                pe.wait_ge(lo_ready, u0 + 3 * c + 2)
                for cols in range(2):
                    down_part(s_before, 0, 0, h_hi, h_lo, False, False, cols)
                turn_hidden(c)
                for cols in range(2):
                    down_part(s_before, 0, 1, h_hi, h_lo, False, False, cols)
                pe.wait_ge(h_lo_ready, c0 + NFC)
                pe.wait_ge(lo_ready, u0 + 3 * NFC)
                for cols in range(2):
                    for k in range(2):
                        last = down_part(s_last, 0, k, last_hi, last_lo, False, k == 1, cols)
                    last.then_inc(sums_done, 1)
                for k in range(2):
                    for cols in range(2):
                        last = down_part(s_before, 1, k, h_hi, h_lo, False, False, cols)
                last.then_inc(w_used, 1)
                for cols in range(2):
                    for k in range(2):
                        last = down_part(s_last, 1, k, last_hi, last_lo, False, k == 1, cols)
                    last.then_inc(sums_done if cols == 0 else w_used, 1)
                if l + 1 < 3:
                    turn_x(l + 1, 0)

            one_unit(8, 1, (6, 7), halves=(0,))
            pe.wait_ge(e_cmp_scaled, 1)
            for hb in range(2):
                for half in range(HALF):
                    at = P * (2 * hb + half)
                    last = nc.tensor.transpose(ps[:, 1, at:at + P],
                                               e_cmp[:, half, 8 * hb:8 * hb + 8, :].rearrange("p n c -> p (n c)"), ident[:, :])
            last.then_inc(e_cmpT_done, 1)
            pe.wait_ge(set_a, KW - 1)
            pe.wait_ge(set_v, KW + 1)
            scores(nsa_job, 0, 0)
            pe.wait_ge(e_cmpT_ready, 1)
            scores(nsa_job, 0, 1)
            one_unit(8, 1, (6, 7), halves=(1,))
            attend(**NSA)
            output_weights(U_WO0, A_X, 0)
            ffn(U_FF0, 0, A_O0, 0)
            for n in range(MOBA_CHUNKS - 1):
                if n == 0:
                    first_chunk(U_MOBA, A_N0, 1)
                else:
                    if n >= 2:
                        pe.wait_ge(evac, NSA_CHUNKS + n - 1)
                    b = MOBA_BANKS[n]
                    chunk(U_MOBA + 2 * n, (b, b + 1))
                if 1 <= n:
                    pe.wait_ge(roped, NSA_CHUNKS - 1 + n)
                    set_free(MQ0 + n - 1)
                    turn_rows(MQ0 + n - 1, (n - 1) % 2)
            scores(moba_job, NSA_JOBS, 0)
            scores(moba_job, NSA_JOBS, 1)
            pe.wait_ge(evac, NSA_CHUNKS + 5)
            chunk(U_MOBA + 2 * 5, (6, 7))
            set_free(MK1 + 1)
            attend(**MOBA)
            output_weights(U_WO1, A_N1, 2)
            ffn(U_FF1, NFC, A_O1, 2)


def _unit(block):
    return block.reshape(-1, P, block.shape[-1]).transpose(1, 0, 2).reshape(P, -1)


def _columns(w, lo, hi):
    return [_unit(w[512 * i:512 * (i + 1), lo:hi]) for i in range(2)]


def _output(w):
    cols = [_columns(w, 512 * c, 512 * (c + 1)) for c in range(2)]
    return [cols[c][tiles] for tiles in range(2) for c in range(2)]


def _network(wg, wu, wd):
    units = []
    for c in range(NFC):
        at = slice(FC * c, FC * (c + 1))
        units += _columns(np.concatenate([wg[:, at], wu[:, at]], axis=1), 0, 2 * FC)
        if c > 0:
            units.append(_unit(wd[FC * (c - 1):FC * c]))
    units.append(_unit(wd[FC * (NFC - 1):]))
    return units


def kernel(x, positions, nsa_w_in, nsa_w_o, nsa_ck_pos, nsa_ck_w1, nsa_ck_w2, nsa_cv_pos, nsa_cv_w1, nsa_cv_w2,
           moba_w_in, moba_w_o, ffn_wg, ffn_wu, ffn_wd, ln1_g, ln1_b, ln2_g, ln2_b):
    import concourse.bacc as bacc
    from concourse.bass_utils import run_bass_kernel_spmd

    a = {k: np.asarray(v) for k, v in locals().items() if k not in ("bacc", "run_bass_kernel_spmd")}
    w_in, w_moba = a["nsa_w_in"][0], a["moba_w_in"][0]
    kv = NH * HD
    part = [w_in[:, kv + 256 * i:kv + 256 * (i + 1)] for i in range(6)]
    chunks = [np.concatenate([part[0], part[1]], axis=1), w_in[:, 0:512], w_in[:, 512:1024],
              np.concatenate([part[2], part[4]], axis=1), np.concatenate([part[3], part[5]], axis=1)]
    units = [u for c in chunks for u in _columns(c, 0, 512)]
    units += _output(a["nsa_w_o"][0])
    units += _network(a["ffn_wg"][0], a["ffn_wu"][0], a["ffn_wd"][0])
    for c in range(MOBA_CHUNKS):
        units += _columns(w_moba, 512 * c, 512 * (c + 1))
    units += _output(a["moba_w_o"][0])
    units += _network(a["ffn_wg"][1], a["ffn_wu"][1], a["ffn_wd"][1])

    def halves(w):
        return w.reshape(2, CS, HD, -1).transpose(0, 2, 1, 3).reshape(P, CS, -1)

    rows = a["x"][0].reshape(HALF, P, D)
    arrays = {
        "x_rows": rows.transpose(1, 0, 2),
        "x_cols": rows.reshape(HALF, P, KT, P).transpose(3, 0, 2, 1).reshape(P, HALF, KT * P),
        "stream": np.stack(units),
        "w_gates": w_in[:, kv + 6 * KV * HD:].reshape(KT, P, 3 * NH).transpose(1, 0, 2),
        "w1": np.stack([halves(a["nsa_ck_w1"][0]), halves(a["nsa_cv_w1"][0])], axis=1),
        "w2": np.stack([a[n][0].reshape(2, P, HD).transpose(1, 0, 2) for n in ("nsa_ck_w2", "nsa_cv_w2")], axis=1),
        "cpos": np.stack([a[n][0].reshape(2, CS, HD).transpose(0, 2, 1).reshape(P, CS)
                          for n in ("nsa_ck_pos", "nsa_cv_pos")], axis=1),
        "positions": a["positions"][0].reshape(HALF, P).transpose(1, 0),
        "norms": np.stack([np.stack([a[f"ln{i}_{p}"][l] for p in "gb"]) for l in range(2) for i in (1, 2)]),
    }
    nc = bacc.Bacc("TRN2", target_bir_lowering=False, num_devices=1)
    ins = {}
    for name, value in arrays.items():
        arrays[name] = np.ascontiguousarray(value)
        ins[name] = nc.dram_tensor(name, arrays[name].shape, mybir.dt.from_np(arrays[name].dtype),
                                   kind="ExternalInput").ap()
    out = nc.dram_tensor("out", [HALF, P, D], mybir.dt.float32, kind="ExternalOutput").ap()
    build(nc, ins["x_rows"], ins["x_cols"], ins["stream"], ins["w_gates"],
          ins["w1"], ins["w2"], ins["cpos"], ins["positions"], ins["norms"], out)
    result = run_bass_kernel_spmd(nc, [arrays], core_ids=[0])
    return result.results[0]["out"].reshape(1, S, D)
```
